# Optimizing a Trainium2 kernel written in Bass

```python
import math
import jax, jax.numpy as jnp
from jax import lax
import numpy as np

D_MODEL = 1024
BATCH = 1
SEQ = 512
DEPTH = 2

NORM_EPS = 1e-6
D_FF = 256 * ((8 * D_MODEL // 3 + 255) // 256)
CHUNK = 64
MIX_W = D_MODEL
M_DH = 64
M_W = MIX_W // 4
M_HEADS = M_W // M_DH
R_DH = 64
R_W = MIX_W // 4
R_HEADS = R_W // R_DH
ROPE_BASE = 10000.0
G_DH = 128
G_W = MIX_W - M_W - R_W
G_HEADS = G_W // G_DH
CONV_K = 4
IN_SIZES = (M_W, M_W, M_W, M_W, M_HEADS, M_HEADS,
            R_W, R_W, R_W, R_W,
            G_W, G_W, G_W, G_W, G_HEADS, G_HEADS)
IN_W = sum(IN_SIZES)


def _rmsnorm(x, gain):
    x32 = x.astype(jnp.float32)
    y = x32 * lax.rsqrt(jnp.mean(x32 * x32, axis=-1, keepdims=True) + NORM_EPS)
    return (y * gain).astype(x.dtype)

def _swiglu(x, w_gate, w_up, w_down):
    hid = jax.nn.silu(jnp.einsum('bsd,df->bsf', x, w_gate)) * jnp.einsum('bsd,df->bsf', x, w_up)
    return jnp.einsum('bsf,fd->bsd', hid, w_down)

def _heads(t, n_heads):
    b, s, w = t.shape
    return t.reshape(b, s, n_heads, w // n_heads).transpose(0, 2, 1, 3)

def _head_rmsnorm(h, gain):
    h = h * lax.rsqrt(jnp.mean(h * h, axis=-1, keepdims=True) + NORM_EPS)
    b, nh, s, d = h.shape
    return h.transpose(0, 2, 1, 3).reshape(b, s, nh * d) * gain

def _l2norm(t):
    return t * lax.rsqrt(jnp.sum(t * t, axis=-1, keepdims=True) + NORM_EPS)

def _rope(t):
    d = t.shape[-1]
    inv_freq = ROPE_BASE ** (-jnp.arange(0, d, 2, dtype=jnp.float32) / d)
    ang = jnp.arange(t.shape[2], dtype=jnp.float32)[:, None] * inv_freq[None, :]
    cos, sin = jnp.cos(ang), jnp.sin(ang)
    t1, t2 = t[..., : d // 2], t[..., d // 2:]
    return jnp.concatenate([t1 * cos - t2 * sin, t1 * sin + t2 * cos], axis=-1)

def _causal_dwconv(x, w):
    k, c = w.shape
    return lax.conv_general_dilated(x, w[:, None, :].astype(x.dtype), window_strides=(1,),
                                    padding=[(k - 1, 0)], dimension_numbers=('NWC', 'WIO', 'NWC'),
                                    feature_group_count=c)

def _to_chunks(t):
    b, h, s = t.shape[:3]
    return jnp.moveaxis(t.reshape(b, h, s // CHUNK, CHUNK, *t.shape[3:]), 2, 0)

def _from_chunks(t):
    n, b, h, l, d = t.shape
    return jnp.moveaxis(t, 0, 2).reshape(b, h, n * l, d)

def _mlstm(q, k, v, i_pre, f_pre):
    b, nh, s, d = q.shape
    k = k * d ** -0.5
    log_f = jax.nn.log_sigmoid(f_pre)
    causal = jnp.tril(jnp.ones((CHUNK, CHUNK), dtype=bool))

    def step(carry, xs):
        c_st, n_st, m_st = carry
        qc, kc, vc, ic, fc = xs
        bcum = jnp.cumsum(fc, axis=-1)
        log_w = jnp.where(causal, bcum[..., :, None] - bcum[..., None, :] + ic[..., None, :], -jnp.inf)
        log_inter = bcum + m_st[..., None]
        m_row = jnp.maximum(log_inter, jnp.max(log_w, axis=-1))
        w = jnp.exp(log_w - m_row[..., None])
        inter = jnp.exp(log_inter - m_row)
        sc = jnp.einsum('bhid,bhjd->bhij', qc, kc) * w
        num = jnp.einsum('bhij,bhje->bhie', sc, vc) + inter[..., None] * jnp.einsum('bhid,bhde->bhie', qc, c_st)
        den = jnp.sum(sc, axis=-1) + inter * jnp.einsum('bhid,bhd->bhi', qc, n_st)
        hc = num / jnp.maximum(jnp.abs(den), jnp.exp(-m_row))[..., None]
        b_last = bcum[..., -1]
        log_src = b_last[..., None] - bcum + ic
        m_new = jnp.maximum(b_last + m_st, jnp.max(log_src, axis=-1))
        carry_decay = jnp.exp(b_last + m_st - m_new)
        kw = kc * jnp.exp(log_src - m_new[..., None])[..., None]
        c_st = carry_decay[..., None, None] * c_st + jnp.einsum('bhjd,bhje->bhde', kw, vc)
        n_st = carry_decay[..., None] * n_st + jnp.sum(kw, axis=2)
        return (c_st, n_st, m_new), hc

    init = (jnp.zeros((b, nh, d, v.shape[-1]), q.dtype), jnp.zeros((b, nh, d), q.dtype),
            jnp.zeros((b, nh), q.dtype))
    _, hs = lax.scan(step, init, (_to_chunks(q), _to_chunks(k), _to_chunks(v),
                                  _to_chunks(i_pre), _to_chunks(log_f)))
    return _from_chunks(hs)

def _retention(q, k, v):
    b, nh, s, d = q.shape
    k = k * d ** -0.5
    log_gamma = jnp.log1p(-jnp.exp2(-5.0 - jnp.arange(nh, dtype=jnp.float32)))
    pos = jnp.arange(CHUNK, dtype=jnp.float32)
    rel = pos[:, None] - pos[None, :]
    causal = rel >= 0
    intra = jnp.where(causal, jnp.exp(jnp.where(causal, rel, 0.0) * log_gamma[:, None, None]), 0.0)
    q_decay = jnp.exp((pos + 1.0) * log_gamma[:, None])[..., None]
    k_decay = jnp.exp((CHUNK - 1.0 - pos) * log_gamma[:, None])[..., None]
    chunk_decay = jnp.exp(CHUNK * log_gamma)[:, None, None]

    def step(r_st, xs):
        qc, kc, vc = xs
        sc = jnp.einsum('bhid,bhjd->bhij', qc, kc) * intra
        o = jnp.einsum('bhij,bhje->bhie', sc, vc) + jnp.einsum('bhid,bhde->bhie', qc * q_decay, r_st)
        r_st = chunk_decay * r_st + jnp.einsum('bhjd,bhje->bhde', kc * k_decay, vc)
        return r_st, o

    init = jnp.zeros((b, nh, d, v.shape[-1]), q.dtype)
    _, outs = lax.scan(step, init, (_to_chunks(q), _to_chunks(k), _to_chunks(v)))
    return _from_chunks(outs)

def _gated_delta(q, k, v, log_alpha, beta):
    b, nh, s, dk = q.shape
    dv = v.shape[-1]
    q = q * dk ** -0.5
    idx = jnp.arange(CHUNK)
    causal = idx[:, None] >= idx[None, :]
    strict = idx[:, None] > idx[None, :]
    eye = jnp.eye(CHUNK, dtype=q.dtype)

    def step(s_st, xs):
        qc, kc, vc, ac, bc = xs
        g = jnp.cumsum(ac, axis=-1)
        diff = g[..., :, None] - g[..., None, :]
        decay = jnp.where(causal, jnp.exp(jnp.where(causal, diff, 0.0)), 0.0)
        kb = kc * bc[..., None]
        a_mat = eye + jnp.where(strict, jnp.einsum('bhid,bhjd->bhij', kb, kc) * decay, 0.0)
        rhs = jnp.concatenate([vc * bc[..., None], kb * jnp.exp(g)[..., None]], axis=-1)
        sol = lax.linalg.triangular_solve(a_mat, rhs, left_side=True, lower=True, unit_diagonal=True)
        u = sol[..., :dv] - jnp.einsum('bhik,bhkv->bhiv', sol[..., dv:], s_st)
        qk = jnp.einsum('bhik,bhjk->bhij', qc, kc) * decay
        o = jnp.einsum('bhik,bhkv->bhiv', qc * jnp.exp(g)[..., None], s_st) + jnp.einsum('bhij,bhjv->bhiv', qk, u)
        g_last = g[..., -1:]
        s_st = jnp.exp(g_last)[..., None] * s_st + jnp.einsum('bhjk,bhjv->bhkv', kc * jnp.exp(g_last - g)[..., None], u)
        return s_st, o

    init = jnp.zeros((b, nh, dk, dv), q.dtype)
    _, outs = lax.scan(step, init, (_to_chunks(q), _to_chunks(k), _to_chunks(v),
                                    _to_chunks(log_alpha), _to_chunks(beta)))
    return _from_chunks(outs)

def _hybrid_mixer(u, w_in, m_i_bias, m_f_bias, g_conv, g_a_log, g_dt_bias,
                  m_out_norm, r_out_norm, g_out_norm, w_out):
    f32 = jnp.float32
    offsets = [int(o) for o in np.cumsum(IN_SIZES)[:-1]]
    proj = jnp.einsum('bsd,dp->bsp', u, w_in).astype(f32)
    (mq, mk, mv, mo, mi, mf, rq, rk, rv, rg, gq, gk, gv, gz, ga, gb) = jnp.split(proj, offsets, axis=-1)
    i_pre = jnp.transpose(mi + m_i_bias, (0, 2, 1))
    f_pre = jnp.transpose(mf + m_f_bias, (0, 2, 1))
    h_m = _mlstm(_heads(mq, M_HEADS), _heads(mk, M_HEADS), _heads(mv, M_HEADS), i_pre, f_pre)
    y_m = _head_rmsnorm(h_m, m_out_norm) * jax.nn.sigmoid(mo)
    h_r = _retention(_rope(_heads(rq, R_HEADS)), _rope(_heads(rk, R_HEADS)), _heads(rv, R_HEADS))
    y_r = _head_rmsnorm(h_r, r_out_norm) * jax.nn.silu(rg)
    qkv = jax.nn.silu(_causal_dwconv(jnp.concatenate([gq, gk, gv], axis=-1), g_conv))
    cq, ck, cv = jnp.split(qkv, 3, axis=-1)
    log_alpha = -jnp.exp(g_a_log) * jax.nn.softplus(ga + g_dt_bias)
    beta = jax.nn.sigmoid(gb)
    h_g = _gated_delta(_l2norm(_heads(cq, G_HEADS)), _l2norm(_heads(ck, G_HEADS)), _heads(cv, G_HEADS),
                       jnp.transpose(log_alpha, (0, 2, 1)), jnp.transpose(beta, (0, 2, 1)))
    y_g = _head_rmsnorm(h_g, g_out_norm) * jax.nn.silu(gz)
    y = jnp.concatenate([y_m, y_r, y_g], axis=-1).astype(u.dtype)
    return jnp.einsum('bsm,md->bsd', y, w_out)

def first_inputs(seed: int = 0) -> dict:
    key = jax.random.key(seed)
    ks = jax.random.split(key, 24)
    f32 = jnp.float32

    def nrm(k, shape, fan_in):
        return jax.random.normal(k, shape, f32) * fan_in ** -0.5

    def gain(k, shape):
        return 1.0 + 0.02 * jax.random.normal(k, shape, f32)

    x = jax.random.normal(ks[0], (BATCH, SEQ, D_MODEL), f32)
    ffn1_norm = gain(ks[1], (DEPTH, D_MODEL))
    ffn1_w_gate = nrm(ks[2], (DEPTH, D_MODEL, D_FF), D_MODEL)
    ffn1_w_up = nrm(ks[3], (DEPTH, D_MODEL, D_FF), D_MODEL)
    ffn1_w_down = nrm(ks[4], (DEPTH, D_FF, D_MODEL), D_FF)
    mix_norm = gain(ks[5], (DEPTH, D_MODEL))
    w_in = nrm(ks[6], (DEPTH, D_MODEL, IN_W), D_MODEL)
    m_i_bias = 0.1 * jax.random.normal(ks[7], (DEPTH, M_HEADS), f32)
    m_f_bias = jnp.linspace(3.0, 6.0, M_HEADS, dtype=f32)[None, :] + 0.1 * jax.random.normal(ks[8], (DEPTH, M_HEADS), f32)
    g_conv = nrm(ks[9], (DEPTH, CONV_K, 3 * G_W), CONV_K)
    g_a_log = jnp.log(jax.random.uniform(ks[10], (DEPTH, G_HEADS), f32, 1.0, 16.0))
    dt = jnp.exp(jax.random.uniform(ks[11], (DEPTH, G_HEADS), f32, math.log(1e-3), math.log(1e-1)))
    g_dt_bias = dt + jnp.log(-jnp.expm1(-dt))
    m_out_norm = gain(ks[12], (DEPTH, M_W))
    r_out_norm = gain(ks[13], (DEPTH, R_W))
    g_out_norm = gain(ks[14], (DEPTH, G_W))
    w_out = nrm(ks[15], (DEPTH, MIX_W, D_MODEL), MIX_W)
    ffn2_norm = gain(ks[16], (DEPTH, D_MODEL))
    ffn2_w_gate = nrm(ks[17], (DEPTH, D_MODEL, D_FF), D_MODEL)
    ffn2_w_up = nrm(ks[18], (DEPTH, D_MODEL, D_FF), D_MODEL)
    ffn2_w_down = nrm(ks[19], (DEPTH, D_FF, D_MODEL), D_FF)
    final_norm = gain(ks[20], (D_MODEL,))
    return {'x': x, 'ffn1_norm': ffn1_norm, 'ffn1_w_gate': ffn1_w_gate, 'ffn1_w_up': ffn1_w_up,
            'ffn1_w_down': ffn1_w_down, 'mix_norm': mix_norm, 'w_in': w_in, 'm_i_bias': m_i_bias,
            'm_f_bias': m_f_bias, 'g_conv': g_conv, 'g_a_log': g_a_log, 'g_dt_bias': g_dt_bias,
            'm_out_norm': m_out_norm, 'r_out_norm': r_out_norm, 'g_out_norm': g_out_norm, 'w_out': w_out,
            'ffn2_norm': ffn2_norm, 'ffn2_w_gate': ffn2_w_gate, 'ffn2_w_up': ffn2_w_up,
            'ffn2_w_down': ffn2_w_down, 'final_norm': final_norm}

def first_block(x, ffn1_norm, ffn1_w_gate, ffn1_w_up, ffn1_w_down, mix_norm, w_in, m_i_bias, m_f_bias,
              g_conv, g_a_log, g_dt_bias, m_out_norm, r_out_norm, g_out_norm, w_out,
              ffn2_norm, ffn2_w_gate, ffn2_w_up, ffn2_w_down, final_norm):
    h = x
    for l in range(DEPTH):
        h = h + 0.5 * _swiglu(_rmsnorm(h, ffn1_norm[l]), ffn1_w_gate[l], ffn1_w_up[l], ffn1_w_down[l])
        h = h + _hybrid_mixer(_rmsnorm(h, mix_norm[l]), w_in[l], m_i_bias[l], m_f_bias[l], g_conv[l],
                              g_a_log[l], g_dt_bias[l], m_out_norm[l], r_out_norm[l], g_out_norm[l], w_out[l])
        h = h + 0.5 * _swiglu(_rmsnorm(h, ffn2_norm[l]), ffn2_w_gate[l], ffn2_w_up[l], ffn2_w_down[l])
    return _rmsnorm(h, final_norm)


DEPTH_2 = 1

SSM_EXPAND = 2
SSM_D_INNER = SSM_EXPAND * D_MODEL
SSM_HEAD_DIM = 64
SSM_HEADS = SSM_D_INNER // SSM_HEAD_DIM
SSM_GROUPS = 4
SSM_HEADS_PER_GROUP = SSM_HEADS // SSM_GROUPS
SSM_D_STATE = 128
SSM_CONV = 4
SSM_CHUNK = 128
SSM_BC_DIM = SSM_GROUPS * SSM_D_STATE
SSM_CONV_DIM = SSM_D_INNER + 2 * SSM_BC_DIM
SSM_NORM_GROUP = SSM_D_INNER // SSM_GROUPS
SSM_DT_MIN = 0.001
SSM_DT_MAX = 0.1

LRU_WIDTH = 1280
LRU_BLOCKS = 10
LRU_BLOCK = LRU_WIDTH // LRU_BLOCKS
LRU_CONV = 4
LRU_C = 8.0

FFN_HIDDEN = -(-8 * D_MODEL // (3 * 256)) * 256

RMS_EPS = 1e-6

N_GATES = 2 * D_MODEL
IN_PROJ_DIM = N_GATES + SSM_D_INNER + SSM_CONV_DIM + SSM_HEADS + 2 * LRU_WIDTH
IN_SPLITS = (
    N_GATES,
    N_GATES + SSM_D_INNER,
    N_GATES + SSM_D_INNER + SSM_CONV_DIM,
    N_GATES + SSM_D_INNER + SSM_CONV_DIM + SSM_HEADS,
    N_GATES + SSM_D_INNER + SSM_CONV_DIM + SSM_HEADS + LRU_WIDTH,
)


def rmsnorm(x, w, eps=RMS_EPS):
    xf = x.astype(jnp.float32)
    y = xf * lax.rsqrt(jnp.mean(xf * xf, axis=-1, keepdims=True) + eps)
    return (y * w.astype(jnp.float32)).astype(x.dtype)

def causal_dwconv(u, w, b):
    k_width = w.shape[0]
    length = u.shape[1]
    up = jnp.pad(u, ((0, 0), (k_width - 1, 0), (0, 0)))
    out = b + up[:, 0:length] * w[0]
    for k in range(1, k_width):
        out = out + up[:, k:k + length] * w[k]
    return out

def segsum_exp(cs):
    t = cs.shape[-1]
    mask = jnp.tril(jnp.ones((t, t), dtype=bool))
    diff = cs[..., :, None] - cs[..., None, :]
    return jnp.exp(jnp.where(mask, diff, -jnp.inf))

def ssd_chunked(xdt, dA, bm, cm):
    b, length, g, r, p = xdt.shape
    n = bm.shape[-1]
    l = SSM_CHUNK
    c = length // l
    xdt = xdt.reshape(b, c, l, g, r, p)
    dA = dA.reshape(b, c, l, g, r)
    bm = bm.reshape(b, c, l, g, n)
    cm = cm.reshape(b, c, l, g, n)

    cs = jnp.cumsum(dA, axis=2)
    lmat = segsum_exp(jnp.moveaxis(cs, 2, -1))
    cb = jnp.einsum('bclgn,bcsgn->bcgls', cm, bm)
    y_diag = jnp.einsum('bcgls,bcgrls,bcsgrp->bclgrp', cb, lmat, xdt)
    decay_states = jnp.exp(cs[:, :, -1:] - cs)
    states = jnp.einsum('bclgn,bclgr,bclgrp->bcgrpn', bm, decay_states, xdt)
    chunk_tot = jnp.moveaxis(cs[:, :, -1], 1, -1)
    chunk_cs = jnp.cumsum(jnp.pad(chunk_tot, ((0, 0), (0, 0), (0, 0), (1, 0))), axis=-1)
    decay_chunk = segsum_exp(chunk_cs)
    states = jnp.concatenate([jnp.zeros_like(states[:, :1]), states], axis=1)
    states_in = jnp.einsum('bgrzc,bcgrpn->bzgrpn', decay_chunk[..., :-1, :], states)
    y_off = jnp.einsum('bclgn,bcgrpn,bclgr->bclgrp', cm, states_in, jnp.exp(cs))
    return (y_diag + y_off).reshape(b, length, g, r, p)

def mamba2_mixer(z, xbc, dt_raw, conv_w, conv_b, dt_bias, a_log, d_skip, norm_w):
    b, length, _ = z.shape
    f32 = jnp.float32
    xbc = jax.nn.silu(causal_dwconv(xbc, conv_w, conv_b))
    xs, bm, cm = jnp.split(xbc, [SSM_D_INNER, SSM_D_INNER + SSM_BC_DIM], axis=-1)
    dt = jax.nn.softplus(dt_raw.astype(f32) + dt_bias.astype(f32))
    a = -jnp.exp(a_log.astype(f32))
    g, r, p, n = SSM_GROUPS, SSM_HEADS_PER_GROUP, SSM_HEAD_DIM, SSM_D_STATE
    xs_h = xs.astype(f32).reshape(b, length, g, r, p)
    dt_h = dt.reshape(b, length, g, r)
    y = ssd_chunked(xs_h * dt_h[..., None], dt_h * a.reshape(g, r),
                    bm.astype(f32).reshape(b, length, g, n),
                    cm.astype(f32).reshape(b, length, g, n))
    y = y + xs_h * d_skip.astype(f32).reshape(g, r, 1)
    y = y.reshape(b, length, SSM_D_INNER) * jax.nn.silu(z.astype(f32))
    yg = y.reshape(b, length, SSM_GROUPS, SSM_NORM_GROUP)
    yg = yg * lax.rsqrt(jnp.mean(yg * yg, axis=-1, keepdims=True) + RMS_EPS)
    y = yg.reshape(b, length, SSM_D_INNER) * norm_w.astype(f32)
    return y.astype(z.dtype)

def rglru_mixer(xl, yl, conv_w, conv_b, w_r, b_r, w_i, b_i, lam):
    b, length, _ = xl.shape
    f32 = jnp.float32
    u = causal_dwconv(xl, conv_w, conv_b)
    ub = u.reshape(b, length, LRU_BLOCKS, LRU_BLOCK)
    r_gate = jax.nn.sigmoid((jnp.einsum('blhi,hij->blhj', ub, w_r).reshape(b, length, LRU_WIDTH) + b_r).astype(f32))
    i_gate = jax.nn.sigmoid((jnp.einsum('blhi,hij->blhj', ub, w_i).reshape(b, length, LRU_WIDTH) + b_i).astype(f32))
    log_a = -LRU_C * r_gate * jax.nn.softplus(-lam.astype(f32))
    a_t = jnp.exp(log_a)
    b_t = jnp.sqrt(-jnp.expm1(2.0 * log_a)) * (i_gate * u.astype(f32))

    def combine(left, right):
        a1, b1 = left
        a2, b2 = right
        return a1 * a2, a2 * b1 + b2

    _, h = lax.associative_scan(combine, (a_t, b_t), axis=1)
    out = h * jax.nn.gelu(yl.astype(f32), approximate=True)
    return out.astype(xl.dtype)

def second_inputs(seed: int = 0) -> dict:
    key = jax.random.key(seed)
    ks = jax.random.split(key, 32)
    f32 = jnp.float32
    nrm = lambda k, shape, scale: jax.random.normal(k, shape, f32) * scale
    L = DEPTH_2

    x = jax.random.normal(ks[0], (BATCH, SEQ, D_MODEL), f32)
    norm1_w = 1.0 + nrm(ks[1], (L, D_MODEL), 0.05)
    w_in = nrm(ks[2], (L, D_MODEL, IN_PROJ_DIM), D_MODEL ** -0.5)
    b_branch_gate = nrm(ks[3], (L, N_GATES), 0.1)

    ssm_conv_w = nrm(ks[4], (L, SSM_CONV, SSM_CONV_DIM), SSM_CONV ** -0.5)
    ssm_conv_b = nrm(ks[5], (L, SSM_CONV_DIM), 0.02)
    u = jax.random.uniform(ks[6], (L, SSM_HEADS), f32)
    dt0 = jnp.exp(u * (math.log(SSM_DT_MAX) - math.log(SSM_DT_MIN)) + math.log(SSM_DT_MIN))
    dt0 = jnp.maximum(dt0, 1e-4)
    ssm_dt_bias = dt0 + jnp.log(-jnp.expm1(-dt0))
    ssm_a_log = jnp.log(jax.random.uniform(ks[7], (L, SSM_HEADS), f32, 1.0, 16.0))
    ssm_d = 1.0 + nrm(ks[8], (L, SSM_HEADS), 0.1)
    ssm_norm_w = 1.0 + nrm(ks[9], (L, SSM_D_INNER), 0.05)
    w_out_ssm = nrm(ks[10], (L, SSM_D_INNER, D_MODEL), SSM_D_INNER ** -0.5)

    lru_conv_w = nrm(ks[11], (L, LRU_CONV, LRU_WIDTH), LRU_CONV ** -0.5)
    lru_conv_b = nrm(ks[12], (L, LRU_WIDTH), 0.02)
    lru_w_r = nrm(ks[13], (L, LRU_BLOCKS, LRU_BLOCK, LRU_BLOCK), LRU_BLOCK ** -0.5)
    lru_b_r = nrm(ks[14], (L, LRU_WIDTH), 0.02)
    lru_w_i = nrm(ks[15], (L, LRU_BLOCKS, LRU_BLOCK, LRU_BLOCK), LRU_BLOCK ** -0.5)
    lru_b_i = nrm(ks[16], (L, LRU_WIDTH), 0.02)
    a0 = jax.random.uniform(ks[17], (L, LRU_WIDTH), f32, 0.9, 0.999)
    s0 = a0 ** (1.0 / LRU_C)
    lru_lambda = jnp.log(s0) - jnp.log1p(-s0)
    w_out_lru = nrm(ks[18], (L, LRU_WIDTH, D_MODEL), LRU_WIDTH ** -0.5)

    w_out = nrm(ks[19], (L, D_MODEL, D_MODEL), D_MODEL ** -0.5)
    norm2_w = 1.0 + nrm(ks[20], (L, D_MODEL), 0.05)
    w_ffn_in = nrm(ks[21], (L, D_MODEL, 2 * FFN_HIDDEN), D_MODEL ** -0.5)
    w_ffn_out = nrm(ks[22], (L, FFN_HIDDEN, D_MODEL), FFN_HIDDEN ** -0.5)
    norm_f_w = 1.0 + nrm(ks[23], (D_MODEL,), 0.05)

    return {
        "x": x, "norm1_w": norm1_w, "w_in": w_in, "b_branch_gate": b_branch_gate,
        "ssm_conv_w": ssm_conv_w, "ssm_conv_b": ssm_conv_b, "ssm_dt_bias": ssm_dt_bias,
        "ssm_a_log": ssm_a_log, "ssm_d": ssm_d, "ssm_norm_w": ssm_norm_w, "w_out_ssm": w_out_ssm,
        "lru_conv_w": lru_conv_w, "lru_conv_b": lru_conv_b, "lru_w_r": lru_w_r, "lru_b_r": lru_b_r,
        "lru_w_i": lru_w_i, "lru_b_i": lru_b_i, "lru_lambda": lru_lambda, "w_out_lru": w_out_lru,
        "w_out": w_out, "norm2_w": norm2_w, "w_ffn_in": w_ffn_in, "w_ffn_out": w_ffn_out,
        "norm_f_w": norm_f_w,
    }

def second_block(x, norm1_w, w_in, b_branch_gate, ssm_conv_w, ssm_conv_b, ssm_dt_bias, ssm_a_log,
              ssm_d, ssm_norm_w, w_out_ssm, lru_conv_w, lru_conv_b, lru_w_r, lru_b_r, lru_w_i,
              lru_b_i, lru_lambda, w_out_lru, w_out, norm2_w, w_ffn_in, w_ffn_out, norm_f_w):
    h = x
    for l in range(DEPTH_2):
        hn = rmsnorm(h, norm1_w[l])
        proj = hn @ w_in[l]
        gates, z, xbc, dt_raw, lru_x, lru_y = jnp.split(proj, IN_SPLITS, axis=-1)
        gates = jax.nn.sigmoid(gates + b_branch_gate[l])
        g_ssm, g_lru = jnp.split(gates, 2, axis=-1)
        y_ssm = mamba2_mixer(z, xbc, dt_raw, ssm_conv_w[l], ssm_conv_b[l], ssm_dt_bias[l],
                             ssm_a_log[l], ssm_d[l], ssm_norm_w[l]) @ w_out_ssm[l]
        y_lru = rglru_mixer(lru_x, lru_y, lru_conv_w[l], lru_conv_b[l], lru_w_r[l], lru_b_r[l],
                            lru_w_i[l], lru_b_i[l], lru_lambda[l]) @ w_out_lru[l]
        h = h + (g_ssm * y_ssm + g_lru * y_lru) @ w_out[l]
        hn = rmsnorm(h, norm2_w[l])
        gate, up = jnp.split(hn @ w_ffn_in[l], 2, axis=-1)
        h = h + (jax.nn.silu(gate) * up) @ w_ffn_out[l]
    return rmsnorm(h, norm_f_w)


def setup_inputs(seed=0):
    out = dict(first_inputs(seed))
    for name, value in second_inputs(seed + 1).items():
        if name != "x":
            out[name + "_2"] = value
    return out


def reference(
    x, ffn1_norm, ffn1_w_gate, ffn1_w_up, ffn1_w_down, mix_norm, w_in, m_i_bias, m_f_bias,
    g_conv, g_a_log, g_dt_bias, m_out_norm, r_out_norm, g_out_norm, w_out, ffn2_norm,
    ffn2_w_gate, ffn2_w_up, ffn2_w_down, final_norm, norm1_w_2, w_in_2, b_branch_gate_2,
    ssm_conv_w_2, ssm_conv_b_2, ssm_dt_bias_2, ssm_a_log_2, ssm_d_2, ssm_norm_w_2, w_out_ssm_2,
    lru_conv_w_2, lru_conv_b_2, lru_w_r_2, lru_b_r_2, lru_w_i_2, lru_b_i_2, lru_lambda_2,
    w_out_lru_2, w_out_2, norm2_w_2, w_ffn_in_2, w_ffn_out_2, norm_f_w_2,
):
    x = first_block(
        x, ffn1_norm, ffn1_w_gate, ffn1_w_up, ffn1_w_down, mix_norm, w_in, m_i_bias, m_f_bias,
        g_conv, g_a_log, g_dt_bias, m_out_norm, r_out_norm, g_out_norm, w_out, ffn2_norm,
        ffn2_w_gate, ffn2_w_up, ffn2_w_down, final_norm,
    )
    return second_block(
        x, norm1_w_2, w_in_2, b_branch_gate_2, ssm_conv_w_2, ssm_conv_b_2, ssm_dt_bias_2,
        ssm_a_log_2, ssm_d_2, ssm_norm_w_2, w_out_ssm_2, lru_conv_w_2, lru_conv_b_2, lru_w_r_2,
        lru_b_r_2, lru_w_i_2, lru_b_i_2, lru_lambda_2, w_out_lru_2, w_out_2, norm2_w_2,
        w_ffn_in_2, w_ffn_out_2, norm_f_w_2,
    )


_drawn_inputs = setup_inputs


def setup_inputs(seed=0):
    import zlib

    import numpy as np

    out = dict(_drawn_inputs(seed))
    spreads = {}
    factors = {'m_i_bias': 64.0,
     'm_out_norm': 6.273,
     'r_out_norm': 5.619,
     'g_out_norm': 4.0,
     'ffn2_norm': 4.186,
     'ssm_conv_b_2': 3.849,
     'lru_b_r_2': 57.633,
     'lru_b_i_2': 33.076}
    for name, (base, spread) in spreads.items():
        noise = np.random.default_rng([zlib.crc32(name.encode()), seed]).standard_normal(out[name].shape)
        drawn = base * np.exp(spread * noise) if base else spread * noise
        out[name] = __import__('jax').numpy.asarray(drawn.astype(out[name].dtype))
    for name, factor in factors.items():
        out[name] = (out[name] * factor).astype(out[name].dtype)
    return out
```

```python
import numpy as np
from contextlib import ExitStack

import concourse.bass as bass
from concourse import mybir

F = mybir.dt.float32
R = mybir.dt.float32r
ACT = mybir.ActivationFunctionType
ALU = mybir.AluOpType

T = 512
D = 1024
NH = 22
EPS = 1e-6
NEG = -3.0e38
OFF = (0, 512, 896, 1152)
QW = 1280
NRAW = 4
NSPL = 4
PACE = (1.2, 0.9, 1.5)

CONSTS, SEL, TABLES, COLS = {}, {}, {}, {}


def number(table, widths):
    at = 0
    for name, width in widths:
        table[name] = (at, width)
        at += width
    return at


NCONST = number(CONSTS, (("ident", 128), ("ones", 2), ("bd64", 128), ("mask", 512), ("lmask", 7 * 128)))
NSEL = number(SEL, (("row", 32), ("pair", 256)))
NROPE = number(TABLES, (("rot", 128), ("cos", 512), ("sin", 512)))
NCOLS = number(COLS, (
    ("ffn1_norm", 16), ("mix_norm", 16), ("ffn2_norm", 16), ("final_norm", 8),
    ("m_out_norm", 4), ("r_out_norm", 4), ("g_out_norm", 8), ("g_conv", 96),
    ("m_i_bias", 2), ("m_f_bias", 2), ("g_a_log", 2), ("g_dt_bias", 2),
    ("norm1_w_2", 8), ("norm2_w_2", 8), ("norm_f_w_2", 8), ("b_branch_gate_2", 16),
    ("ssm_conv_w_2", 96), ("ssm_conv_b_2", 24), ("ssm_dt_bias_2", 1), ("ssm_a_log_2", 1),
    ("ssm_d_2", 16), ("ssm_norm_w_2", 16), ("lru_conv_w_2", 40), ("lru_conv_b_2", 10),
    ("lru_b_r_2", 10), ("lru_b_i_2", 10), ("lru_lambda_2", 10), ("eps", 1)))
NSMALL = 392

TMP = (45, 46, 47, 48)
RSTD = 49
M_Y, M_G, M_BETA, M_HEAD = 0, 8, 9, (10, 21)
M_Q, M_K, M_V, M_D, M_NG, M_EM = 32, 34, 36, 40, 43, 44
M_ROWS = 32
S_ACC, S_CS, S_X, S_Z, S_XP, S_B, S_C, S_CB, S_D = 0, 8, (9, 17), (13, 21), 25, 33, 34, 35, (38, 41)
L_Y, L_U, L_YL, L_UH, L_R, L_I = 9, (29, 31), (33, 35), 37, 41, 43

B_PROJ, B_MISC, B_ATT, B_LONG, B_SUM = (0, 1), (2, 3, 4), 5, (6, 7), 7


def drain(steps):
    while True:
        try:
            next(steps)
        except StopIteration as end:
            return end.value


class Engine:

    def __init__(self, sem):
        self.sem, self.n, self.todo, self.waited = sem, 0, [], {}

    def wait(self, *marks):
        for sem, value in marks:
            if self.waited.get(id(sem), 0) >= value:
                continue
            self.waited[id(sem)] = value
            self.todo.append(lambda e, sem=sem, value=value: e.wait_ge(sem, value))

    def put(self, make):
        self.todo.append(make)

    def mark(self, make):
        self.n += 1
        self.todo.append(lambda e: make(e).then_inc(self.sem, 1))
        return (self.sem, self.n)

    def here(self):
        return (self.sem, self.n)

    def run(self, e):
        for f in self.todo:
            f(e)


class Scalar(Engine):
    def act(self, out, in_, fn, **kw):
        return self.mark(lambda e: e.activation(out, in_, fn, **kw))

    def copy(self, out, in_, **kw):
        return self.act(out, in_, ACT.Copy, **kw)


class Vector(Engine):
    def tt(self, out, a, b, op):
        return self.mark(lambda e: e.tensor_tensor(out, a, b, op))

    def stt(self, out, a, s, b, op0, op1):
        return self.mark(lambda e: e.scalar_tensor_tensor(out=out, in0=a, scalar=s, in1=b, op0=op0, op1=op1))

    def ts(self, out, a, s1, op0, s2=None, op1=None):
        if op1 is None:
            return self.mark(lambda e: e.tensor_scalar(out, a, s1, None, op0))
        return self.mark(lambda e: e.tensor_scalar(out, a, s1, s2, op0, op1))

    def scan(self, out, d0, d1, op0, op1):
        return self.mark(lambda e: e.tensor_tensor_scan(out, d0, d1, 0.0, op0, op1))

    def recip(self, t):
        return self.mark(lambda e: e.reciprocal(t, t))

    def copy(self, out, in_):
        return self.mark(lambda e: e.tensor_copy(out, in_))

    def own(self):
        self.wait(self.here())


class Tensor(Engine):
    def mm(self, out, lhsT, rhs, start, stop):
        self.put(lambda e: e.matmul(out, lhsT, rhs, start=start, stop=stop))

    def mm_mark(self, out, lhsT, rhs, start, stop):
        return self.mark(lambda e: e.matmul(out, lhsT, rhs, start=start, stop=stop))

    def mm_share(self, out, lhsT, rhs, start, stop, last):
        make = lambda e: e.matmul(out, lhsT, rhs, start=start, stop=stop, skip_group_check=True)
        return self.mark(make) if last else self.put(make)

    def mm3(self, out, a, b, start, stop, last):
        (ah, al), (bh, bl) = a, b
        self.mm(out, ah, bh, start, False)
        self.mm(out, ah, bl, False, False)
        if last:
            return self.mm_mark(out, al, bh, False, stop)
        return self.mm(out, al, bh, False, stop)

    def turn(self, out, in_, ident):
        self.put(lambda e: e.transpose(out, in_, ident))

    def turn_mark(self, out, in_, ident):
        return self.mark(lambda e: e.transpose(out, in_, ident))


class Kernel:
    def __init__(self, nc, ins, out, ctx):
        self.nc, self.I, self.out = nc, ins, out
        self.units = plan_units(ins)
        sem = lambda n: ctx.enter_context(nc.semaphore(n))
        self.P, self.A, self.V = Tensor(sem("s_pe")), Scalar(sem("s_act")), Vector(sem("s_dve"))
        self.G, self.S = Engine(sem("s_pool")), Engine(sem("s_sp"))
        self.s_raw = [sem(f"s_raw{i}") for i in range(NRAW)]
        self.s_load = {n: sem(f"s_{n}") for n in ("x0", "x1", "x2", "x3", "cst", "sel", "col", "gw", "rope",
                                                  "ret0", "ret1")}
        self.n_load = {n: 0 for n in self.s_load}
        self.s_out = sem("s_out")
        self.at = -(-nc.sbuf_base // 64) * 64

        def place(name, width, dt=F):
            t = nc.alloc_sbuf_tensor_at(name, [128, width], dt, offset=self.at)
            self.at += -(-width * 4 // 64) * 64
            return t

        self.h = [place(f"h{i}", T) for i in range(8)]
        self.hn = [(place(f"hnh{i}", T, R), place(f"hnl{i}", T, R)) for i in range(8)]
        self.raw = [place(f"raw{i}", 1024) for i in range(NRAW)]
        self.spl = [(place(f"wh{i}", 1024, R), place(f"wl{i}", 1024, R)) for i in range(NSPL)]
        self.cst = place("cst", NCONST)
        self.selr = place("selr", NSEL, R)
        self.col = place("col", NCOLS)
        self.small = place("small", NSMALL)
        self.n_small = 0
        self.base = self.at
        assert self.base + 50 * 2048 <= nc.sbuf_usable_end, (nc.sbuf_usable_end - self.base) / 2048
        self.placed = {}
        self.ps = [ctx.enter_context(nc.psum_tensor(f"ps{i}", [128, T], F)) for i in range(8)]
        self.bank_read = [[] for _ in range(8)]
        self.tmp_read = [[] for _ in range(4)]
        self.n_proj = self.n_misc = self.n_tmp = 0
        self.h_ready = [[] for _ in range(8)]
        self.hn_ready = [[] for _ in range(8)]
        self.split_done, self.unit_done = [], []
        self.work, self.pace, self.due = [], 0.0, 0.0
        self.late = None

    def at_slot(self, i, n=1, dt=F):
        key = (i, n, "r" if dt == R else "f")
        if key not in self.placed:
            self.placed[key] = self.nc.alloc_sbuf_tensor_at(
                f"m{key[2]}{i}_{n}", [128, 512 * n], dt, offset=self.base + 2048 * i)
        return self.placed[key]

    def columns_for(self, n):
        self.n_small += n
        assert self.n_small <= NSMALL
        return self.small[:, self.n_small - n:self.n_small]

    def c(self, name, a=0, b=None, rows=128):
        o, w = CONSTS[name]
        return self.cst[0:rows, o + a:o + (w if b is None else b)]

    def cl(self, name, i=0, n=1, rows=128):
        o, _ = COLS[name]
        return self.col[0:rows, o + i:o + i + n]

    def next_tmp(self):
        self.n_tmp += 1
        k = self.n_tmp % 4
        return k, self.at_slot(TMP[k])

    def next_misc(self):
        self.n_misc += 1
        return B_MISC[self.n_misc % 3]

    def load(self, name, dst, src):
        self.n_load[name] += 16
        self.G.put(lambda e: e.dma_start(dst, src).then_inc(self.s_load[name], 16))
        return (self.s_load[name], self.n_load[name])

    def fence(self):
        ends = (self.P.here(), self.A.here(), self.V.here())
        for q in (self.A, self.V, self.G):
            q.wait(*ends)

    def step(self):
        g = self.work.pop(0)
        if next(g, "end") != "end":
            self.work.append(g)

    def beside(self, n=1):
        self.due += n * self.pace
        while self.due >= 1.0:
            self.due -= 1.0
            if self.work:
                self.step()

    def finish(self):
        while self.work:
            self.step()

    def fetch(self, u):
        src, n = self.units[u]
        raw = self.raw[u % NRAW]
        if u >= NRAW:
            self.S.wait(*self.split_done[u - NRAW])
        self.S.put(lambda e: e.dma_start(raw[:, 0:n], src).then_inc(self.s_raw[u % NRAW], 16))

    def split(self, u):
        _, n = self.units[u]
        raw, (hi, lo) = self.raw[u % NRAW], self.spl[u % NSPL]
        landed = (self.s_raw[u % NRAW], 16 * (u // NRAW + 1))
        self.A.wait(landed)
        if u >= NSPL:
            self.A.wait(self.unit_done[u - NSPL])
        high = self.A.copy(hi[:, 0:n], raw[:, 0:n])
        self.V.wait(landed, high)
        if u >= NSPL:
            self.V.wait(self.unit_done[u - NSPL])
        low = self.V.tt(lo[:, 0:n], raw[:, 0:n], hi[:, 0:n].bitcast(F), ALU.subtract)
        self.split_done.append((high, low))
        if u + NRAW < len(self.units):
            self.fetch(u + NRAW)

    def unit(self):
        u = len(self.unit_done)
        hi, lo = self.spl[u % NSPL]
        n = self.units[u][1]
        self.P.wait(*self.split_done[u])
        v = lambda t: t[:, 0:n].rearrange("p (k c) -> p k c", c=128)
        return v(hi), v(lo)

    def unit_used(self, done):
        self.unit_done.append(done)
        u = len(self.split_done)
        if u < len(self.units):
            self.split(u)

    def product(self, bank, xs, ready):
        self.P.wait(*self.bank_read[bank])
        nk = len(xs)
        for k0 in range(0, nk, 8):
            wh, wl = self.unit()
            kn = min(8, nk - k0)
            for k in range(kn):
                if k % 2 == 0:
                    self.beside()
                self.P.wait(*ready[k0 + k])
                done = self.P.mm3(self.ps[bank][:, :], (wh[:, k, :], wl[:, k, :]),
                                  (xs[k0 + k][0][:, :], xs[k0 + k][1][:, :]),
                                  k0 + k == 0, k0 + k == nk - 1, k == kn - 1)
            self.unit_used(done)
        return done

    def proj(self, n, xs, ready, take):
        for i in range(n):
            bank = B_PROJ[self.n_proj % 2]
            self.n_proj += 1
            done = self.product(bank, xs, ready)
            self.run_late()
            self.bank_read[bank] = take(i, self.ps[bank], done)

    def proj_h(self, n, take):
        self.proj(n, self.hn, self.hn_ready, take)

    def proj_tokens(self, take):
        bank = B_PROJ[self.n_proj % 2]
        self.n_proj += 1
        self.P.wait(*self.bank_read[bank])
        wh, wl = self.unit()
        for j in range(4):
            js = slice(128 * j, 128 * j + 128)
            for k in range(8):
                self.P.wait(*self.hn_ready[k])
                done = self.P.mm3(self.ps[bank][:, js], (self.hn[k][0][:, js], self.hn[k][1][:, js]),
                                  (wh[:, k, :], wl[:, k, :]), k == 0, k == 7, j == 3 and k == 7)
        self.unit_used(done)
        self.bank_read[bank] = take(self.ps[bank], done)
        self.beside(4)

    def split_tile(self, src, hi, lo, ready):
        self.A.wait(ready)
        high = self.A.copy(hi, src)
        self.V.wait(high, ready)
        low = self.V.tt(lo, src, hi.bitcast(F), ALU.subtract)
        return [high, low]

    def h_new(self, i, done, gain):
        self.h_ready[i] = [done]
        kx, x = self.next_tmp()
        self.V.wait(*self.tmp_read[kx], done)
        scaled = self.V.ts(x[:, :], self.h[i][:, :], self.cl(gain[0], gain[1] + i), ALU.mult)
        hi, lo = self.hn[i]
        self.A.wait(self.hn_last)
        self.V.wait(self.hn_last)
        self.hn_ready[i] = self.split_tile(x[:, :], hi[:, :], lo[:, :], scaled)
        self.tmp_read[kx] = self.hn_ready[i]
        ks, sq = self.next_tmp()
        self.A.wait(*self.tmp_read[ks], done)
        squared = self.A.act(sq[:, :], self.h[i][:, :], ACT.Square)

        def later():
            self.P.wait(squared, *self.bank_read[B_SUM])
            for j in range(4):
                m = self.P.mm_share(self.ps[B_SUM][:, j:j + 1], sq[:, 128 * j:128 * j + 128],
                                    self.c("ones", 0, 1), i == 0 and j == 0, i == 7, j == 3)
            self.tmp_read[ks] = [m]
            self.sum_done = m
            if i == 7:
                self.h_rstd()

        self.late = later

    def rstd_columns(self, bank, cols, n, done, eps=EPS):
        self.A.wait(done, *self.col_read)
        root = self.A.act(cols, bank[:, 0:4], ACT.Sqrt, bias=self.cl("eps"), scale=1.0 / n)
        self.V.wait(root)
        return root, self.V.recip(cols)

    def rows_of(self, out, cols, ready):
        self.P.wait(ready)
        for j in range(4):
            put = self.P.mm_mark if j == 3 else self.P.mm
            m = put(out[:, 128 * j:128 * j + 128], cols[:, j:j + 1].to_broadcast([128, 128]),
                    self.c("ident"), True, True)
        return m

    def h_rstd(self):
        root, cols = self.rstd_columns(self.ps[B_SUM], self.rc, D, self.sum_done)
        self.bank_read[B_SUM] = [root]
        b = self.next_misc()
        self.P.wait(*self.bank_read[b])
        spread = self.rows_of(self.ps[b], self.rc, cols)
        self.V.wait(spread)
        self.rs_ready = self.V.copy(self.rs[:, :], self.ps[b][:, :])
        self.bank_read[b] = [self.rs_ready]
        self.rc_ready = cols

    def run_late(self):
        if self.late:
            self.late()
            self.late = None

    def norm_ready(self):
        self.run_late()
        self.V.wait(self.rs_ready)

    def add_h(self, scale, gain):
        def take(i, bank, done):
            self.V.wait(done, *self.h_ready[i])
            m = self.V.stt(self.h[i][:, :], bank[:, :], scale, self.h[i][:, :], ALU.mult, ALU.add)
            self.h_new(i, m, gain)
            return [m]
        return take

    def ffn(self, scale, gain):
        self.norm_ready()
        self.fence()
        hid = [(self.at_slot(2 * i, dt=R), self.at_slot(2 * i + 1, dt=R)) for i in range(NH)]
        ready = [[] for _ in range(NH)]
        held = []

        def gate(i, bank, done):
            k, g = self.next_tmp()
            self.V.wait(done, *self.tmp_read[k])
            m = self.V.tt(g[:, :], bank[:, :], self.rs[:, :], ALU.mult)
            self.A.wait(m)
            held.append((k, g, self.A.act(g[:, :], g[:, :], ACT.Silu)))
            return [m]

        def up(i, bank, done):
            k, g, silu = held.pop()
            self.V.wait(silu, done)
            m = self.V.tt(g[:, :], g[:, :], self.rs[:, :], ALU.mult)
            self.V.wait(m)
            both = self.V.tt(g[:, :], g[:, :], bank[:, :], ALU.mult)
            ready[i] = self.split_tile(g[:, :], hid[i][0][:, :], hid[i][1][:, :], both)
            self.tmp_read[k] = ready[i]
            return [both]

        for i in range(NH):
            self.proj_h(1, gate)
            self.proj_h(1, lambda _, b, d, i=i: up(i, b, d))
        self.hn_last = self.P.here()
        self.proj(8, hid, ready, self.add_h(scale, gain))

    def softplus(self, out, x, t1, t2, t3, ready):
        A, V = self.A, self.V
        A.wait(ready)
        a = A.act(t1, x, ACT.Abs)
        A.wait(a)
        e = A.act(t1, t1, ACT.Exp, scale=-1.0)
        V.wait(e)
        u = V.ts(t2, t1, 1.0, ALU.add)
        A.wait(u)
        ln = A.act(t3, t2, ACT.Ln)
        V.wait(u)
        m = V.stt(t1, t2, -1.0, t1, ALU.add, ALU.subtract)
        yield
        V.wait(ln, m)
        V.recip(t2)
        V.own()
        V.tt(t1, t1, t2, ALU.mult)
        V.own()
        V.tt(t3, t3, t1, ALU.subtract)
        V.own()
        return V.stt(out, x, 0.0, t3, ALU.max, ALU.add)

    def split_rows(self, dst, rows, n, ready):
        self.A.wait(ready)
        if n < 32:
            self.G.wait(ready)
            z = self.G.mark(lambda e: e.memset(dst[0:64, :].bitcast(F), 0.0))
            self.A.wait(z)
            self.V.wait(z)
        hi = self.A.copy(dst[0:n, :], rows)
        self.V.wait(hi, ready)
        return self.V.tt(dst[32:32 + n, :], rows, dst[0:n, :].bitcast(F), ALU.subtract)

    def spread(self, rows, h, ready):
        b = self.next_misc()
        self.P.wait(ready, *self.bank_read[b])
        return b, self.P.mm_mark(self.ps[b][:, :], self.selr[0:64, h:h + 1].to_broadcast([64, 128]),
                                 rows[0:64, :], True, True)

    def spread_pair(self, rows, h, ready):
        b = self.next_misc()
        self.P.wait(ready, *self.bank_read[b])
        return b, self.P.mm_mark(self.ps[b][:, :], self.selr[0:64, 32 + 64 * h:160 + 64 * h],
                                 rows[0:64, :], True, True)

    def columns(self, dst, rows, n, ready):
        b = self.next_misc()
        self.P.wait(ready, *self.bank_read[b])
        for j in range(4):
            turn = self.P.turn_mark if j == 3 else self.P.turn
            t = turn(self.ps[b][:, n * j:n * j + n], rows[:, 128 * j:128 * j + 128], self.c("ident", 0, n, rows=n))
        self.V.wait(t)
        m = self.V.copy(dst, self.ps[b][:, 0:4 * n])
        self.bank_read[b] = [m]
        return m

    def decay(self, b, spread, col, out):
        self.V.wait(spread)
        for jt in range(4):
            w = T - 128 * jt
            m = self.V.stt(out[:, OFF[jt]:OFF[jt] + w], self.ps[b][:, 128 * jt:T], col(jt), self.c("mask", 0, w),
                           ALU.subtract, ALU.min)
        self.bank_read[b] = [m]
        self.A.wait(m)
        return self.A.act(out[:, 0:QW], out[:, 0:QW], ACT.Exp)

    def turn_tile(self, src, ready):
        b = self.next_misc()
        self.P.wait(*ready, *self.bank_read[b])
        for j in range(4):
            js = slice(128 * j, 128 * j + 128)
            turn = self.P.turn_mark if j == 3 else self.P.turn
            t = turn(self.ps[b][:, js], src[:, js], self.c("ident"))
        return b, t

    def keep(self, dst, got, scale=None, fn=None):
        def take(i, bank, done):
            d = dst(i)
            self.V.wait(done)
            if scale is None:
                m = self.V.tt(d[:, :], bank[:, :], self.rs[:, :], ALU.mult)
            else:
                m = self.V.stt(d[:, :], bank[:, :], scale, self.rs[:, :], ALU.mult, ALU.mult)
            got[i] = m
            if fn is not None:
                self.A.wait(m)
                got[i] = fn(d, i)
            return [m]
        return take

    def conv(self, dst, got, w, bias=None):
        def take(i, bank, done):
            k0, x = self.next_tmp()
            s = dst(i)
            self.V.wait(done, *self.tmp_read[k0])
            m = self.V.tt(x[:, :], bank[:, :], self.rs[:, :], ALU.mult)
            self.A.wait(m)
            if bias is None:
                a = self.A.copy(s[:, :], x[:, :], scale=w(i, 3))
            else:
                a = self.A.act(s[:, :], x[:, :], ACT.Identity, scale=w(i, 3), bias=bias(i))
            self.V.wait(a)
            for k in (2, 1, 0):
                d = 3 - k
                self.V.own()
                c = self.V.stt(s[:, d:T], x[:, 0:T - d], w(i, k), s[:, d:T], ALU.mult, ALU.add)
            self.tmp_read[k0] = [c]
            got[i] = c
            return [m]
        return take

    def silu(self, x, ready):
        self.A.wait(ready)
        return self.A.act(x[:, :], x[:, :], ACT.Silu)

    def rms_of(self, x, ready, n, cols):
        k, sq = self.next_tmp()
        self.A.wait(ready, *self.tmp_read[k])
        s = self.A.act(sq[:, :], x[:, :], ACT.Square)
        b = self.next_misc()
        self.P.wait(s, *self.bank_read[b])
        for j in range(4):
            put = self.P.mm_mark if j == 3 else self.P.mm
            m = put(self.ps[b][:, j:j + 1], sq[:, 128 * j:128 * j + 128], self.c("ones", 0, 1), True, True)
        self.tmp_read[k] = [m]
        root, ready = self.rstd_columns(self.ps[b], cols, n, m)
        self.bank_read[b] = [root]
        b = self.next_misc()
        self.P.wait(*self.bank_read[b])
        return b, self.rows_of(self.ps[b], cols, ready)

    def gated_norm(self, o, ready, gain, y, gate, b, spread):
        self.V.wait(ready, spread)
        m = self.V.stt(o[:, :], o[:, :], gain, self.ps[b][:, :], ALU.mult, ALU.mult)
        self.bank_read[b] = [m]
        self.V.wait(gate, m)
        return self.V.tt(y[:, :], o[:, :], y[:, :], ALU.mult)

    def half_norm(self, o, ready, gain, y, gate):
        k, sq = self.next_tmp()
        self.A.wait(ready, *self.tmp_read[k])
        s = self.A.act(sq[:, :], o[:, :], ACT.Square)
        b = self.next_misc()
        self.P.wait(s, *self.bank_read[b])
        m = self.P.mm_mark(self.ps[b][:, :], self.c("bd64"), sq[:, :], True, True)
        self.A.wait(m)
        root = self.A.act(sq[:, :], self.ps[b][:, :], ACT.Sqrt, bias=self.cl("eps"), scale=1.0 / 64)
        self.bank_read[b] = [root]
        self.V.wait(root)
        r = self.V.recip(sq[:, :])
        self.V.wait(r, ready)
        m = self.V.stt(o[:, :], o[:, :], gain, sq[:, :], ALU.mult, ALU.mult)
        self.tmp_read[k] = [m]
        self.V.wait(gate, m)
        return self.V.tt(y[:, :], o[:, :], y[:, :], ALU.mult)

    def load_rows(self, src):
        raw = self.at_slot(M_ROWS + 8, 2)
        hi, lo = self.at_slot(M_ROWS + 10, 2, R), self.at_slot(M_ROWS, 2, R)
        landed = self.load("gw", raw[:, :], src)
        yield
        self.rows_split = self.split_tile(raw[:, :], hi[:, :], lo[:, :], landed)
        yield
        self.P.wait(*self.rows_split, *self.bank_read[B_ATT])
        for k in range(8):
            ks = slice(128 * k, 128 * k + 128)
            self.P.wait(*self.hn_ready[k])
            m = self.P.mm3(self.ps[B_ATT][:, :], (hi[:, ks], lo[:, ks]), (self.hn[k][0][:, :], self.hn[k][1][:, :]),
                           k == 0, k == 7, k == 7)
        yield
        return m

    def rows(self, l):
        P, A, V, G, I = self.P, self.A, self.V, self.G, self.I
        done = yield from self.load_rows(I["gate_w"][l])
        rows = [self.at_slot(M_ROWS + q) for q in range(4)]
        ri, rf, ra, rb = (r[0:4, :] for r in rows)
        t1, t2, t3, t4 = (self.at_slot(M_ROWS + 4 + q)[0:4, :] for q in range(4))
        V.wait(done)
        for q, r in enumerate((ri, rf, ra, rb)):
            got = V.tt(r, self.ps[B_ATT][32 * q:32 * q + 4, :], self.rs[32 * q:32 * q + 4, :], ALU.mult)
        self.bank_read[B_ATT] = [got]
        V.own()
        a = V.ts(ra, ra, self.cl("g_dt_bias", l, rows=4), ALU.add)
        sp = yield from self.softplus(ra, ra, t1, t2, t4, a)
        A.wait(sp)
        ea = A.act(self.one_col[0:4, :], self.cl("g_a_log", l, rows=4), ACT.Exp)
        G.wait(sp)
        ones = G.mark(lambda e: e.memset(t1, 1.0))
        V.wait(ea, sp)
        la = V.ts(ra, ra, self.one_col[0:4, :], ALU.mult, -1.0, ALU.mult)
        V.wait(ones, la)
        for j in range(4):
            js = slice(128 * j, 128 * j + 128)
            g = V.scan(t2[:, js], t1[:, js], ra[:, js], ALU.mult, ALU.add)
        yield
        self.g_ready = self.split_rows(self.at_slot(M_G, dt=R), t2, 4, g)
        self.g_cols_ready = self.columns(self.g_cols, t2, 4, g)
        yield
        A.wait(got)
        beta = A.act(rb, rb, ACT.Sigmoid)
        self.b_ready = self.split_rows(self.at_slot(M_BETA, dt=R), rb, 4, beta)
        self.b_cols_ready = self.columns(self.b_cols, rb, 4, beta)
        yield
        V.ts(ri, ri, self.cl("m_i_bias", l, rows=4), ALU.add)
        f = V.ts(rf, rf, self.cl("m_f_bias", l, rows=4), ALU.add, -1.0, ALU.mult)
        V.wait(self.g_ready, self.g_cols_ready)
        A.wait(self.g_ready, self.g_cols_ready)
        f = yield from self.softplus(rf, rf, t1, t2, t3, f)
        G.wait(f)
        ones = G.mark(lambda e: e.memset(t1, 1.0))
        V.wait(ones, f)
        V.scan(t2, t1, rf, ALU.mult, ALU.subtract)
        V.own()
        na = V.tt(rf, t2, ri, ALU.subtract)
        G.wait(na)
        zero = G.mark(lambda e: e.memset(t1, 0.0))
        yield
        self.a_cols_ready = self.columns(self.m_cols, rf, 4, na)
        V.wait(na)
        a = V.ts(ri, rf, -1.0, ALU.mult)
        V.wait(zero, a)
        V.scan(t3, ri, t1, ALU.max, ALU.add)
        V.own()
        m = V.tt(t2, t2, t3, ALU.add)
        A.wait(m)
        em = A.act(t2, t2, ACT.Exp, scale=-1.0)
        yield
        ng = V.ts(t3, t3, -1.0, ALU.mult)
        self.em_ready = self.split_rows(self.at_slot(M_EM, dt=R), t2, 4, em)
        self.ng_ready = self.split_rows(self.at_slot(M_NG, dt=R), t3, 4, ng)
        self.rows_end = [P.here(), A.here(), V.here()]

    def mixer(self, l, gain):
        P, A, V = self.P, self.A, self.V
        self.norm_ready()
        self.fence()
        y = [self.at_slot(M_Y + i) for i in range(8)]
        y_ready = [None] * 8
        self.pace = 0.5
        self.gate_ready = {}
        self.work.append(self.rows(l))
        self.delta_qkv(l, 0)
        self.finish()
        self.pace = PACE[0]
        self.work += [self.delta(l, h, h, y, y_ready) for h in (0, 1)]
        q, k, v = self.qkv()
        self.gates(y, 0, ACT.Sigmoid)
        self.gates(y, 4, ACT.Silu)
        self.finish()
        A.wait(P.here(), V.here())
        V.wait(P.here(), A.here())
        self.pace = PACE[1]
        self.work.append(self.mlstm(l, q, k, v, y, y_ready))
        self.delta_qkv(l, 2)
        self.finish()
        self.pace = PACE[2]
        self.work += [self.delta(l, h, h - 2, y, y_ready) for h in (2, 3)]
        q, k, v = self.qkv(rope=True)
        self.work.append(self.retention(l, q, k, v, y, y_ready))
        self.gates(y, 2, ACT.Silu)
        self.gates(y, 6, ACT.Silu)
        self.hn_last = P.here()
        self.finish()
        self.pace = 0.0
        A.wait(P.here(), V.here())
        V.wait(P.here(), A.here())
        parts = [(self.at_slot(M_HEAD[0] + 2 * i, dt=R), self.at_slot(M_HEAD[0] + 2 * i + 1, dt=R)) for i in range(8)]
        split = [self.split_tile(y[i][:, :], parts[i][0][:, :], parts[i][1][:, :], y_ready[i]) for i in range(8)]
        self.proj(8, parts, split, self.add_h(1.0, gain))

    def gates(self, y, i0, fn):
        def after(d, i):
            m = self.A.act(d[:, :], d[:, :], fn)
            self.gate_ready[i0 + i] = m
            return m
        self.proj_h(2, self.keep(lambda i: y[i0 + i], {}, fn=after))

    def qkv(self, rope=False):
        P, A, V, G = self.P, self.A, self.V, self.G
        q, k = [self.at_slot(M_Q + i) for i in range(2)], [self.at_slot(M_K + i) for i in range(2)]
        v = [self.at_slot(M_V + i) for i in range(4)]
        for e in (V, G, A):
            e.wait(*self.rows_end)
        qm, km, vm = {}, {}, {}
        if rope:
            tab = self.at_slot(M_D, 3)
            tab_ready = self.load("rope", tab[:, 0:NROPE], self.I["rope"])
        for j in range(4):
            zero = G.mark(lambda e, j=j: e.memset(v[j][:, :], 0.0 if rope else 1.0))
        self.proj_h(2, self.keep(lambda i: q[i], qm))
        self.proj_h(2, self.keep(lambda i: k[i], km, scale=0.125))
        for n in range(2):
            def take(bank, done):
                V.wait(done, zero, self.rc_ready)
                for j in range(4):
                    for s in range(2):
                        o = 256 * n + 128 * s + 64 * s
                        m = V.ts(v[j][:, o:o + 64], bank[:, 128 * j + 64 * s:128 * j + 64 * s + 64],
                                 self.rc[:, j:j + 1], ALU.mult)
                vm[n] = m
                return [m]
            self.proj_tokens(take)
        if rope:
            tb = lambda n: tab[:, TABLES[n][0]:TABLES[n][0] + TABLES[n][1]]
            for ready, x in ((qm, q), (km, k)):
                for i in range(2):
                    b = self.next_misc()
                    P.wait(ready[i], tab_ready, *self.bank_read[b])
                    m = P.mm_mark(self.ps[b][:, :], tb("rot"), x[i][:, :], True, True)
                    kt, r = self.next_tmp()
                    V.wait(m, tab_ready, *self.tmp_read[kt])
                    s = V.tt(r[:, :], self.ps[b][:, :], tb("sin"), ALU.mult)
                    self.bank_read[b] = [s]
                    V.tt(x[i][:, :], x[i][:, :], tb("cos"), ALU.mult)
                    V.own()
                    ready[i] = V.tt(x[i][:, :], x[i][:, :], r[:, :], ALU.add)
                    self.tmp_read[kt] = [ready[i]]
        return (q, qm), (k, km), (v, vm)

    def attend(self, h, q, k, v, weigh):
        P = self.P
        (qt, qm), (kt, km), (vt, vm) = q, k, v
        p, pr = h // 2, slice(64 * (h % 2), 64 * (h % 2) + 64)
        out = self.ps[B_ATT]
        got = []

        def score(jt):
            w = T - 128 * jt
            b = self.next_misc()
            P.wait(qm[p], km[p], *self.bank_read[b])
            m = P.mm_mark(self.ps[b][:, 0:w], kt[p][pr, 128 * jt:128 * jt + 128], qt[p][pr, 128 * jt:T], True, True)
            self.V.wait(m)
            got.append(weigh(jt, self.ps[b][:, 0:w], w))
            self.bank_read[b] = [got[-1][1]]

        def values(jt):
            place, m = got[jt]
            P.wait(m, vm[0], vm[1], *self.bank_read[B_ATT])
            return P.mm_mark(out[:, 128 * jt:T], vt[jt][:, 128 * h:128 * h + 128], place, jt == 0, jt == 3)

        score(0)
        score(1)
        yield
        score(2)
        score(3)
        values(0)
        values(1)
        yield
        values(2)
        return values(3)

    def mlstm(self, l, q, k, v, y, y_ready):
        P, A, V = self.P, self.A, self.V
        d = self.at_slot(M_D, 3)
        att = [P.here()]
        for p in range(2):
            o, den = self.at_slot(M_Q + p), self.at_slot(M_K + p)
            for s in range(2):
                h = 2 * p + s
                b, spread = self.spread(self.at_slot(M_NG, dt=R), h, self.ng_ready)
                V.wait(self.a_cols_ready, *att)
                w_ready = self.decay(b, spread, lambda jt: self.m_cols[:, 4 * jt + h:4 * jt + h + 1], d)
                yield
                V.wait(w_ready)

                def weigh(jt, scores, w):
                    place = d[:, OFF[jt]:OFF[jt] + w]
                    return place, V.tt(place, scores, place, ALU.mult)

                done = yield from self.attend(h, q, k, v, weigh)
                att = [done]
                num, dn = slice(64 * s, 64 * s + 64), slice(64 - 64 * s, 128 - 64 * s)
                A.wait(done)
                n = A.copy(o[num, :], self.ps[B_ATT][num, :])
                a = A.act(den[num, :], self.ps[B_ATT][dn, :], ACT.Abs)
                self.bank_read[B_ATT] = [a]
                yield
            b, spread = self.spread_pair(self.at_slot(M_EM, dt=R), 2 * p, self.em_ready)
            V.wait(a, spread)
            m = V.tt(den[:, :], den[:, :], self.ps[b][:, :], ALU.max)
            self.bank_read[b] = [m]
            V.own()
            V.recip(den[:, :])
            V.own()
            m = V.tt(o[:, :], o[:, :], den[:, :], ALU.mult)
            yield
            y_ready[p] = self.half_norm(o, m, self.cl("m_out_norm", 2 * l + p), y[p], self.gate_ready[p])
            yield
        self.rows_end = [P.here(), A.here(), V.here()]

    def retention(self, l, q, k, v, y, y_ready):
        P, A, V, G = self.P, self.A, self.V, self.G
        d = self.at_slot(M_D, 3)
        att = [P.here(), V.here()]
        ret_read = [[P.here(), V.here()], [P.here(), V.here()]]
        for p in range(2):
            o = self.at_slot(M_Q + p)
            for s in range(2):
                h = 2 * p + s
                tab = self.at_slot((M_NG, M_EM)[s])
                G.wait(*ret_read[s])
                tab_ready = self.load(f"ret{s}", tab[:, :], self.I["ret"][h])
                V.wait(tab_ready, *att)

                def weigh(jt, scores, w):
                    place = d[:, OFF[jt]:OFF[jt] + w]
                    return place, V.tt(place, scores, tab[:, 0:w], ALU.mult)

                done = yield from self.attend(h, q, k, v, weigh)
                att = [done]
                ret_read[s] = [V.here()]
                num = slice(64 * s, 64 * s + 64)
                A.wait(done)
                m = A.copy(o[num, :], self.ps[B_ATT][num, :])
                self.bank_read[B_ATT] = [m]
                yield
            while 2 + p not in self.gate_ready:
                yield
            y_ready[2 + p] = self.half_norm(o, m, self.cl("r_out_norm", 2 * l + p), y[2 + p], self.gate_ready[2 + p])
            yield

    def delta_qkv(self, l, h0):
        self.qkv_ready = {}
        for kind in range(3):
            got = {}
            self.proj_h(2, self.conv(lambda i: self.at_slot(M_HEAD[i] + kind), got,
                                     lambda i, k: self.cl("g_conv", 48 * l + 12 * k + 4 * kind + h0 + i)))
            for i in range(2):
                self.qkv_ready[kind, i] = self.silu(self.at_slot(M_HEAD[i] + kind), got[i])

    def delta(self, l, h, i, y, y_ready):
        P, A, V = self.P, self.A, self.V
        at = [self.at_slot(M_HEAD[i] + n) for n in range(11)]
        Q, K, vt, eg, et, kbT, vb, kd, kb, pt, Z = at
        X, am, St, o, Y, U, wt = K, vt, vt, et, kbT, kbT, kb
        four = [slice(128 * c, 128 * c + 128) for c in range(4)]
        blk = lambda t: t[:, :].rearrange("p (c n) -> p c n", c=4)
        of_head = lambda t: t.rearrange("p (c h) -> p h c", h=4)[:, h, :]
        wide = lambda t: t.unsqueeze(2).to_broadcast([128, 4, 128])
        sd = self.d_cols[i]
        q_ready, k_ready, v_ready = (self.qkv_ready[n, i] for n in range(3))
        ps = self.ps
        norm = {}
        for x, ready, s in ((Q, q_ready, 128.0 ** -0.5), (K, k_ready, 1.0)):
            b, spread = self.rms_of(x, ready, 1, sd[:, 8:12])
            V.wait(spread, ready)
            norm[s] = V.stt(x[:, :], x[:, :], s, ps[b][:, :], ALU.mult, ALU.mult)
            self.bank_read[b] = [norm[s]]
            self.col_read = [P.here()]
            yield
        q_ready, k_ready = norm[128.0 ** -0.5], norm[1.0]
        b, t = self.turn_tile(vt, [v_ready])
        V.wait(t, self.b_cols_ready)
        vb_ready = V.tt(blk(vb), blk(ps[b]), wide(of_head(self.b_cols)), ALU.mult)
        self.bank_read[b] = [vb_ready]
        v_turned = t
        b, spread = self.spread(self.at_slot(M_G, dt=R), h, self.g_ready)
        A.wait(spread)
        eg_ready = A.act(eg[:, :], ps[b][:, :], ACT.Exp)
        V.wait(spread, eg_ready, self.g_cols_ready)
        for c in range(4):
            m = V.stt(et[:, four[c]], ps[b][:, four[c]], self.g_cols[:, 4 * c + h:4 * c + h + 1],
                      self.c("mask", 0, 128), ALU.subtract, ALU.min)
        A.wait(m)
        et_ready = A.act(et[:, :], et[:, :], ACT.Exp)
        last_g = V.tt(sd[:, 0:4], ps[b][:, 127::128], of_head(self.g_cols), ALU.subtract)
        self.bank_read[b] = [last_g]
        A.wait(last_g, self.g_cols_ready)
        kd_col = A.act(sd[:, 0:4], sd[:, 0:4], ACT.Exp)
        kb_col = A.act(sd[:, 4:8], of_head(self.g_cols), ACT.Exp)
        V.wait(kb_col)
        kb_col = V.tt(sd[:, 4:8], sd[:, 4:8], of_head(self.b_cols), ALU.mult)
        yield
        b, spread = self.spread(self.at_slot(M_BETA, dt=R), h, self.b_ready)
        V.wait(spread, k_ready)
        kbT_ready = V.tt(kbT[:, :], K[:, :], ps[b][:, :], ALU.mult)
        self.bank_read[b] = [kbT_ready]
        b, t = self.turn_tile(K, [k_ready])
        V.wait(t, kd_col, kb_col)
        kd_ready = V.tt(blk(kd), blk(ps[b]), wide(sd[:, 0:4]), ALU.mult)
        kb_ready = V.tt(blk(kb), blk(ps[b]), wide(sd[:, 4:8]), ALU.mult)
        self.bank_read[b] = [kb_ready]
        yield
        b = self.next_misc()
        P.wait(k_ready, q_ready, *self.bank_read[b])
        for c in range(4):
            put = P.mm_mark if c == 3 else P.mm
            m = put(ps[b][:, four[c]], K[:, four[c]], Q[:, four[c]], True, True)
        V.wait(m, et_ready)
        pt_ready = V.tt(pt[:, :], ps[b][:, :], et[:, :], ALU.mult)
        self.bank_read[b] = [pt_ready]
        b = self.next_misc()
        P.wait(kbT_ready, *self.bank_read[b])
        for c in range(4):
            put = P.mm_mark if c == 3 else P.mm
            k_read = put(ps[b][:, four[c]], K[:, four[c]], kbT[:, four[c]], True, True)
        V.wait(k_read)
        a_ready = V.tt(et[:, :], ps[b][:, :], et[:, :], ALU.mult)
        self.bank_read[b] = [a_ready]
        V.wait(eg_ready)
        qg_ready = V.tt(Q[:, :], Q[:, :], eg[:, :], ALU.mult)
        yield
        lm = lambda s: self.c("lmask", 128 * s, 128 * s + 128).unsqueeze(1).to_broadcast([128, 4, 128])
        V.wait(a_ready, v_turned)
        m = V.tt(blk(am), blk(et), lm(0), ALU.mult)
        V.wait(m)
        z_ready = V.tt(blk(Z), self.c("ident").unsqueeze(1).to_broadcast([128, 4, 128]), blk(am), ALU.subtract)
        b, t = self.turn_tile(Z, [z_ready])
        A.wait(t, k_read, k_ready)
        x_ready = A.copy(X[:, :], ps[b][:, :])
        self.bank_read[b] = [x_ready]
        am_read, y_read = z_ready, k_read
        yield
        for s in range(1, 7):
            V.wait(am_read)
            am_ready = V.tt(blk(am), blk(et), lm(s), ALU.mult)
            b = self.next_misc()
            P.wait(am_ready, x_ready, *self.bank_read[b])
            for c in range(4):
                put = P.mm_mark if c == 3 else P.mm
                am_read = put(ps[b][:, four[c]], am[:, four[c]], X[:, four[c]], True, True)
            A.wait(am_read, y_read)
            y_ready_ = A.copy(Y[:, :], ps[b][:, :])
            self.bank_read[b] = [y_ready_]
            yield
            b = self.next_misc()
            P.wait(y_ready_, z_ready, *self.bank_read[b])
            for c in range(4):
                put = P.mm_mark if c == 3 else P.mm
                m = put(ps[b][:, four[c]], Y[:, four[c]], Z[:, four[c]], True, True)
            y_read = m
            bz = b
            if s < 6:
                b = self.next_misc()
                P.wait(*self.bank_read[b])
                for c in range(4):
                    put = P.mm_mark if c == 3 else P.mm
                    m = put(ps[b][:, four[c]], Z[:, four[c]], Y[:, four[c]], True, True)
                y_read = m
                V.wait(m, x_ready)
                x_ready = V.tt(X[:, :], X[:, :], ps[b][:, :], ALU.subtract)
                self.bank_read[b] = [x_ready]
            V.wait(y_read, z_ready)
            z_ready = V.tt(Z[:, :], Z[:, :], ps[bz][:, :], ALU.subtract)
            self.bank_read[bz] = [z_ready]
            yield
        b = self.next_misc()
        P.wait(kb_ready, z_ready, *self.bank_read[b])
        for c in range(4):
            put = P.mm_mark if c == 3 else P.mm
            m = put(ps[b][:, four[c]], kb[:, four[c]], Z[:, four[c]], True, True)
        A.wait(m, kb_ready)
        wt_ready = A.copy(wt[:, :], ps[b][:, :], scale=-1.0)
        self.bank_read[b] = [wt_ready]
        yield
        ob = B_LONG[i]
        s_ready = None
        for c in range(4):
            b = self.next_misc()
            P.wait(vb_ready, z_ready, *self.bank_read[b])
            if c == 0:
                m = P.mm_mark(ps[b][:, 0:128], Z[:, four[c]], vb[:, four[c]], True, True)
            else:
                P.mm(ps[b][:, 0:128], Z[:, four[c]], vb[:, four[c]], True, False)
                P.wait(wt_ready, s_ready)
                m = P.mm_mark(ps[b][:, 0:128], wt[:, four[c]], St[:, 0:128], False, True)
            A.wait(m, y_read)
            u_ready = A.copy(U[:, four[c]], ps[b][:, 0:128])
            self.bank_read[b] = [u_ready]
            P.wait(u_ready, pt_ready, *self.bank_read[ob])
            if c == 0:
                o_done = P.mm_mark(ps[ob][:, four[c]], U[:, four[c]], pt[:, four[c]], True, True)
            else:
                P.wait(qg_ready)
                P.mm(ps[ob][:, four[c]], U[:, four[c]], pt[:, four[c]], True, False)
                o_done = P.mm_mark(ps[ob][:, four[c]], St[:, 0:128], Q[:, four[c]], False, True)
            if c < 3:
                b = self.next_misc()
                P.wait(kd_ready, *self.bank_read[b])
                m = P.mm_mark(ps[b][:, 0:128], kd[:, four[c]], U[:, four[c]], True, True)
                V.wait(m)
                if c:
                    V.wait(s_ready, o_done, eg_ready)
                    s_ready = V.stt(St[:, 0:128], St[:, 0:128], eg[:, 128 * c + 127:128 * c + 128],
                                    ps[b][:, 0:128], ALU.mult, ALU.add)
                else:
                    V.wait(am_read)
                    s_ready = V.copy(St[:, 0:128], ps[b][:, 0:128])
                self.bank_read[b] = [s_ready]
            yield
        while 4 + h not in self.gate_ready:
            yield
        A.wait(o_done, am_ready)
        m = A.copy(o[:, :], ps[ob][:, :])
        self.bank_read[ob] = [m]
        b, spread = self.rms_of(o, m, 128, sd[:, 8:12])
        self.col_read = [P.here()]
        y_ready[4 + h] = self.gated_norm(o, m, self.cl("g_out_norm", 4 * l + h), y[4 + h],
                                         self.gate_ready[4 + h], b, spread)

    def second(self, gain):
        P, A, V, G, I = self.P, self.A, self.V, self.G, self.I
        self.norm_ready()
        self.fence()
        def rows():
            done = yield from self.load_rows(I["dt_w"])
            dt, da, t1, t2, t3 = (self.at_slot(M_ROWS + n)[0:32, :] for n in range(5))
            V.wait(done)
            m = V.tt(dt, self.ps[B_ATT][0:32, :], self.rs[0:32, :], ALU.mult)
            self.bank_read[B_ATT] = [m]
            V.own()
            m = V.ts(dt, dt, self.cl("ssm_dt_bias_2", rows=32), ALU.add)
            sp = yield from self.softplus(dt, dt, t1, t2, t3, m)
            ea = A.act(self.one_col[0:32, :], self.cl("ssm_a_log_2", rows=32), ACT.Exp)
            G.wait(sp)
            ones = G.mark(lambda e: e.memset(t1, 1.0))
            V.wait(ea, sp)
            V.ts(da, dt, self.one_col[0:32, :], ALU.mult, -1.0, ALU.mult)
            V.wait(ones)
            V.own()
            cs = V.scan(t2, t1, da, ALU.mult, ALU.add)
            yield
            cs_ready = self.split_rows(cs_rows, t2, 32, cs)
            dt_ready = self.columns(dt_cols, dt, 32, sp)
            cc_ready = self.columns(cs_cols, t2, 32, cs)
            return cs_ready, dt_ready, cc_ready

        cs_rows = self.at_slot(S_CS, dt=R)
        dt_cols, cs_cols = self.columns_for(128), self.columns_for(128)
        cs_ready, dt_ready, cc_ready = drain(rows())
        ends = [P.here(), A.here(), V.here()]
        for e in (A, V, G):
            e.wait(*ends)

        acc = [self.at_slot(S_ACC + i) for i in range(8)]
        self.acc_ready = [None] * 8
        x = [[self.at_slot(S_X[s] + i) for i in range(4)] for s in range(2)]
        z = [[self.at_slot(S_Z[s] + i) for i in range(4)] for s in range(2)]
        B, C, cb = self.at_slot(S_B), self.at_slot(S_C), self.at_slot(S_CB, 3)
        xp = [self.at_slot(S_XP + 2 * j, 2) for j in range(4)]
        for j in range(4):
            xp_zero = G.mark(lambda e, j=j: e.memset(xp[j][:, :], 0.0))
        bc_read = []
        out_read = [[], []]
        x_ready, z_ready, y_ready = {}, {}, {}

        def load_bcx(g):
            got = {}
            for i, (t, name) in enumerate(((B, 16 + g), (C, 20 + g))):
                A.wait(*bc_read)
                self.proj_h(1, self.conv(lambda _: t, got, lambda _, k: self.cl("ssm_conv_w_2", 24 * k + name),
                                         lambda _: self.cl("ssm_conv_b_2", name)))
                x_ready["B" if i == 0 else "C"] = self.silu(t, got[0])
            A.wait(*out_read[g % 2])
            s = g % 2
            for i in range(4):
                self.proj_h(1, self.conv(lambda _: x[s][i], got,
                                         lambda _, k: self.cl("ssm_conv_w_2", 24 * k + 4 * g + i),
                                         lambda _: self.cl("ssm_conv_b_2", 4 * g + i)))
                x_ready[i] = self.silu(x[s][i], got[0])

        def prepare(g):
            nonlocal bc_read
            for jt in range(4):
                w = T - 128 * jt
                b = self.next_misc()
                P.wait(x_ready["B"], x_ready["C"], *self.bank_read[b])
                m = P.mm_mark(self.ps[b][:, 0:w], B[:, 128 * jt:128 * jt + 128], C[:, 128 * jt:T], True, True)
                A.wait(m, V.here())
                cb_ready = A.copy(cb[:, OFF[jt]:OFF[jt] + w], self.ps[b][:, 0:w])
                self.bank_read[b] = [cb_ready]
            bc_read = [m]
            V.wait(xp_zero, dt_ready, P.here())
            for i in range(4):
                b, t = self.turn_tile(x[g % 2][i], [x_ready[i]])
                V.wait(t)
                for j in range(4):
                    for q in range(2):
                        h = 2 * i + q
                        a = 32 * j + 8 * g + h
                        m = V.ts(xp[j][:, 128 * h + 64 * q:128 * h + 64 * q + 64],
                                 self.ps[b][:, 128 * j + 64 * q:128 * j + 64 * q + 64], dt_cols[:, a:a + 1], ALU.mult)
                self.bank_read[b] = [m]
            return cb_ready, m

        def heads(g, cb_ready, xp_ready, xr):
            s = g % 2
            d = [self.at_slot(S_D[q], 3) for q in range(2)]
            d_read = [[], []]
            bank = self.ps[B_ATT]
            put_off = []

            def weights(h):
                b, spread = self.spread(cs_rows, 8 * g + h, cs_ready)
                V.wait(cc_ready, *d_read[h % 2])
                e = self.decay(b, spread, lambda jt: cs_cols[:, 32 * jt + 8 * g + h:32 * jt + 8 * g + h + 1],
                               d[h % 2])
                V.wait(e, cb_ready)
                return V.tt(d[h % 2][:, 0:QW], d[h % 2][:, 0:QW], cb[:, 0:QW], ALU.mult)

            def gated(i, t, v):
                V.wait(v, z_ready[i])
                v = V.tt(t[:, :], t[:, :], z[s][i][:, :], ALU.mult)
                k, sq = self.next_tmp()
                A.wait(v, *self.tmp_read[k])
                a = A.act(sq[:, :], t[:, :], ACT.Square)
                P.wait(a, *self.bank_read[B_LONG[0]])
                for j in range(4):
                    n = P.mm_share(self.ps[B_LONG[0]][:, j:j + 1], sq[:, 128 * j:128 * j + 128],
                                   self.c("ones", 0, 1), i == 0 and j == 0, i == 3, j == 3)
                self.tmp_read[k] = [n]
                return n

            w = weights(0)
            yield
            for h in range(8):
                i, q = h // 2, h % 2
                after = weights(h + 1) if h < 7 else None
                if put_off and put_off[0][0] in z_ready:
                    gated(*put_off.pop(0))
                P.wait(w, xp_ready, *self.bank_read[B_ATT])
                for jt in range(4):
                    put = P.mm_mark if jt == 3 else P.mm
                    m = put(bank[:, 128 * jt:T], xp[jt][:, 128 * h:128 * h + 128],
                            d[q][:, OFF[jt]:OFF[jt] + T - 128 * jt], q == 0 and jt == 0, q == 1 and jt == 3)
                d_read[q] = [m]
                w = after
                if q:
                    t = x[s][i]
                    V.wait(m, xr[i])
                    v = V.stt(t[:, :], t[:, :], self.cl("ssm_d_2", 4 * g + i), bank[:, :], ALU.mult, ALU.add)
                    self.bank_read[B_ATT] = [v]
                    put_off.append((i, t, v))
                yield
            while put_off:
                while put_off[0][0] not in z_ready:
                    yield
                n = gated(*put_off.pop(0))
                yield
            cols = self.d_cols[0][:, 8:12]
            root, ready = self.rstd_columns(self.ps[B_LONG[0]], cols, 512, n)
            self.bank_read[B_LONG[0]] = [root]
            b = self.next_misc()
            P.wait(*self.bank_read[b])
            spread = self.rows_of(self.ps[b], cols, ready)
            self.col_read = [spread]
            V.wait(spread)
            for i in range(4):
                t = x[s][i]
                v = V.stt(t[:, :], t[:, :], self.cl("ssm_norm_w_2", 4 * g + i), self.ps[b][:, :], ALU.mult, ALU.mult)
                hi, lo = self.at_slot(S_Z[s] + i, dt=R), self.at_slot(S_X[s] + i, dt=R)
                y_ready[g, i] = self.split_tile(t[:, :], hi[:, :], lo[:, :], v)
            self.bank_read[b] = [v]

        def out(g):
            s = g % 2
            xs = [(self.at_slot(S_Z[s] + i, dt=R), self.at_slot(S_X[s] + i, dt=R)) for i in range(4)]

            def take(i, bank, done):
                V.wait(done)
                if g == 0:
                    m = V.copy(acc[i][:, :], bank[:, :])
                else:
                    V.wait(self.acc_ready[i])
                    m = V.tt(acc[i][:, :], acc[i][:, :], bank[:, :], ALU.add)
                self.acc_ready[i] = m
                if g < 3:
                    return [m]
                V.wait(m, gate_ready[i])
                self.acc_ready[i] = V.tt(acc[i][:, :], acc[i][:, :], gate[i][:, :], ALU.mult)
                return [m]

            self.proj(8, xs, [y_ready[g, i] for i in range(4)], take)
            out_read[s] = [P.here()]

        load_bcx(0)
        self.pace = 0.3
        for g in range(4):
            ready = prepare(g)
            z_ready.clear()
            self.work.append(heads(g, *ready, [x_ready[i] for i in range(4)]))
            V.wait(*out_read[g % 2])
            self.proj_h(4, self.keep(lambda i: z[g % 2][i], z_ready,
                                     fn=lambda d, i: A.act(d[:, :], d[:, :], ACT.Silu)))
            if g:
                out(g - 1)
            if g < 3:
                load_bcx(g + 1)
            else:
                gate, gate_ready = [*x[0], *z[0]], {}
                V.wait(*out_read[0])
                self.proj_h(8, self.keep(lambda i: gate[i], gate_ready, fn=lambda d, i: A.act(
                    d[:, :], d[:, :], ACT.Sigmoid, bias=self.cl("b_branch_gate_2", i))))
            self.finish()
        self.pace = 0.0
        out(3)
        self.lru(acc, gain)

    def lru(self, acc, gain):
        P, A, V = self.P, self.A, self.V
        self.fence()
        lam = self.columns_for(50)
        L = lambda j: lam[:, 10 * j:10 * j + 10]
        m = V.ts(L(0), self.cl("lru_lambda_2", 0, 10), -1.0, ALU.mult)
        drain(self.softplus(L(4), L(0), L(1), L(2), L(3), m))
        V.own()
        lam_ready = V.ts(L(0), L(4), 8.0, ALU.mult)
        V.wait(lam_ready)
        y = [(self.at_slot(L_Y + 2 * i, dt=R), self.at_slot(L_Y + 2 * i + 1, dt=R)) for i in range(10)]
        y_ready = [None] * 10
        r = [self.at_slot(L_R + i) for i in range(2)]
        gi = [self.at_slot(L_I + i) for i in range(2)]
        ends = [[], []]

        def scans(p, u, yl, yl_ready, g_ready, split):
            two = range(2)
            th, sq, tanh, a2, iu = {}, {}, {}, {}, {}
            for i in two:
                k = 2 * p + i
                th[i], sq[i] = self.next_tmp(), self.next_tmp()
                V.wait(g_ready[0, i])
                m = V.ts(r[i][:, :], r[i][:, :], lam[:, k:k + 1], ALU.mult)
                A.wait(m, *self.tmp_read[th[i][0]], *self.tmp_read[sq[i][0]])
                tanh[i] = A.act(th[i][1][:, :], r[i][:, :], ACT.Tanh)
                a = A.act(r[i][:, :], r[i][:, :], ACT.Exp, scale=-1.0)
                A.wait(a)
                a2[i] = A.act(sq[i][1][:, :], r[i][:, :], ACT.Square)
                V.wait(g_ready[1, i], *split[i])
                iu[i] = V.tt(gi[i][:, :], gi[i][:, :], u[i][:, :], ALU.mult)
            root = {}
            for i in two:
                t = th[i][1]
                V.wait(a2[i], tanh[i])
                m = V.stt(t[:, :], sq[i][1][:, :], 1.0, t[:, :], ALU.add, ALU.mult)
                self.tmp_read[sq[i][0]] = [m]
                A.wait(m)
                root[i] = A.act(t[:, :], t[:, :], ACT.Sqrt)
            for i in two:
                V.wait(root[i], iu[i])
                b = V.tt(gi[i][:, :], gi[i][:, :], th[i][1][:, :], ALU.mult)
                self.tmp_read[th[i][0]] = [b]
            yield
            for i in two:
                k = 2 * p + i
                V.own()
                h = V.scan(u[i][:, :], r[i][:, :], gi[i][:, :], ALU.mult, ALU.add)
                V.wait(h, yl_ready[i])
                m = V.tt(u[i][:, :], u[i][:, :], yl[i][:, :], ALU.mult)
                y_ready[k] = self.split_tile(u[i][:, :], y[k][0][:, :], y[k][1][:, :], m)
                yield
            ends[p % 2] = [V.here(), A.here()]

        uh = [(self.at_slot(L_UH + 2 * i, dt=R), self.at_slot(L_UH + 2 * i + 1, dt=R)) for i in range(2)]
        uh_read = []

        def gates(p, u, yl, yl_ready, split):
            nonlocal uh_read
            g_ready = {}
            for n, (dst, bias) in enumerate(((r, "lru_b_r_2"), (gi, "lru_b_i_2"))):
                wh, wl = self.unit()
                for i in range(2):
                    b = self.next_misc()
                    P.wait(*split[i], *self.bank_read[b])
                    m = P.mm3(self.ps[b][:, :], (wh[:, i, :], wl[:, i, :]), (uh[i][0][:, :], uh[i][1][:, :]),
                              True, True, True)
                    A.wait(m, *ends[1 - p % 2])
                    g_ready[n, i] = A.act(dst[i][:, :], self.ps[b][:, :], ACT.Sigmoid,
                                          bias=self.cl(bias, 2 * p + i))
                    self.bank_read[b] = [g_ready[n, i]]
                self.unit_used(m)
            uh_read = [m]
            self.work.append(scans(p, u, yl, yl_ready, g_ready, split))

        last = None
        self.pace = 0.25
        for p in range(5):
            s = p % 2
            u = [self.at_slot(L_U[s] + i) for i in range(2)]
            yl = [self.at_slot(L_YL[s] + i) for i in range(2)]
            A.wait(*ends[s])
            V.wait(*ends[s])
            got, yl_ready, split = {}, {}, {}
            self.proj_h(2, self.conv(lambda i: u[i], got, lambda i, k: self.cl("lru_conv_w_2", 10 * k + 2 * p + i),
                                     lambda i: self.cl("lru_conv_b_2", 2 * p + i)))
            self.finish()
            if last:
                gates(*last)
            A.wait(*uh_read)
            V.wait(*uh_read)
            for i in range(2):
                split[i] = self.split_tile(u[i][:, :], uh[i][0][:, :], uh[i][1][:, :], got[i])
            self.proj_h(2, self.keep(lambda i: yl[i], yl_ready, fn=lambda d, i: A.act(
                d[:, :], d[:, :], ACT.Gelu_apprx_tanh)))
            last = (p, u, yl, yl_ready, split)
        self.finish()
        gates(*last)
        self.pace = 0.0
        gate = [self.at_slot(L_U[0] + i) for i in range(8)]
        gate_ready = {}
        self.finish()
        V.wait(P.here(), A.here())
        self.proj_h(8, self.keep(lambda i: gate[i], gate_ready, fn=lambda d, i: A.act(
            d[:, :], d[:, :], ACT.Sigmoid, bias=self.cl("b_branch_gate_2", 8 + i))))
        self.hn_last = P.here()
        parts = [(self.at_slot(L_UH + i, dt=R), self.at_slot(L_U[0] + i, dt=R)) for i in range(8)]
        split = [None] * 8

        def take(i, bank, done):
            V.wait(done, gate_ready[i])
            m = V.tt(gate[i][:, :], gate[i][:, :], bank[:, :], ALU.mult)
            V.wait(m, self.acc_ready[i])
            c = V.tt(acc[i][:, :], acc[i][:, :], gate[i][:, :], ALU.add)
            split[i] = self.split_tile(acc[i][:, :], parts[i][0][:, :], parts[i][1][:, :], c)
            return [m]

        self.proj(8, y, y_ready, take)
        self.proj(8, parts, split, self.add_h(1.0, gain))

    def build(self):
        P, A, V, G, S, I = self.P, self.A, self.V, self.G, self.S, self.I
        for u in range(NRAW):
            self.fetch(u)
        self.rs, self.rc = self.at_slot(RSTD), self.columns_for(4)
        self.m_cols, self.g_cols, self.b_cols = (self.columns_for(16) for _ in range(3))
        self.one_col = self.columns_for(1)
        self.d_cols = [self.columns_for(12) for _ in range(2)]
        self.col_read, self.gate_ready = [], {}
        x = [self.at_slot(2 * j, 2) for j in range(4)]
        xt = [self.load(f"x{j}", x[j][:, :], I["x"][128 * j:128 * j + 128, :]) for j in range(4)]
        cst_ready = self.load("cst", self.cst[:, :], I["consts"])
        col_ready = self.load("col", self.col[:, :], I["cols"])
        sel_ready = self.load("sel", self.at_slot(8)[:, 0:NSEL], I["sel"])
        for q in (P, A, V):
            q.wait(cst_ready, col_ready)
        A.wait(sel_ready)
        sel_ready = A.copy(self.selr[:, :], self.at_slot(8)[:, 0:NSEL])
        P.wait(sel_ready)
        self.hn_last = sel_ready
        for u in range(NSPL):
            self.split(u)
        gain = ("ffn1_norm", 0)
        P.wait(*xt)
        for i in range(8):
            b = B_MISC[i % 3]
            P.wait(*self.bank_read[b])
            for j in range(4):
                turn = P.turn_mark if j == 3 else P.turn
                t = turn(self.ps[b][:, 128 * j:128 * j + 128], x[j][:, 128 * i:128 * i + 128], self.c("ident"))
            V.wait(t)
            v = V.copy(self.h[i][:, :], self.ps[b][:, :])
            self.bank_read[b] = [v]
            self.h_new(i, v, gain)
            self.run_late()
        for l in range(2):
            self.ffn(0.5, ("mix_norm", 8 * l))
            self.mixer(l, ("ffn2_norm", 8 * l))
            self.ffn(0.5, ("ffn1_norm", 8) if l == 0 else ("final_norm", 0))
        self.norm_h()
        for i in range(8):
            self.h_new(i, self.h_ready[i][0], ("norm1_w_2", 0))
            self.run_late()
        self.second(("norm2_w_2", 0))
        self.ffn(1.0, ("norm_f_w_2", 0))
        self.norm_h("norm_f_w_2")
        self.fence()
        for j in range(4):
            o = self.at_slot(2 * j, 2)
            for half in range(2):
                b = self.next_misc()
                P.wait(*self.bank_read[b])
                for i in range(4):
                    k = 4 * half + i
                    P.wait(*self.h_ready[k])
                    turn = P.turn_mark if i == 3 else P.turn
                    t = turn(self.ps[b][:, 128 * i:128 * i + 128], self.h[k][:, 128 * j:128 * j + 128],
                             self.c("ident"))
                if half:
                    A.wait(t)
                    self.bank_read[b] = [A.copy(o[:, 512:1024], self.ps[b][:, :])]
                else:
                    V.wait(t)
                    self.bank_read[b] = [V.copy(o[:, 0:512], self.ps[b][:, :])]
            S.wait(A.here(), V.here())
            S.put(lambda e, o=o, j=j: e.dma_start(self.out[128 * j:128 * j + 128, :], o[:, :]).then_inc(self.s_out, 16))
        S.wait((self.s_out, 64))

    def norm_h(self, name="final_norm"):
        self.norm_ready()
        for i in range(8):
            self.V.wait(*self.h_ready[i])
            self.h_ready[i] = [self.V.stt(self.h[i][:, :], self.h[i][:, :], self.cl(name, i), self.rs[:, :],
                                          ALU.mult, ALU.mult)]


def plan_units(ins):
    out = []

    def tiles(w, first, n):
        for i in range(first, first + n):
            width = w.shape[2]
            for a in range(0, width, 1024):
                b = min(a + 1024, width)
                out.append((w[i, :, a:b], b - a))

    def ffn(wg, g0, wu, u0, wd):
        for i in range(NH):
            tiles(wg, g0 + i, 1)
            tiles(wu, u0 + i, 1)
        tiles(wd, 0, 8)

    for l in range(2):
        ffn(ins["ffn1_w_gate"][l], 0, ins["ffn1_w_up"][l], 0, ins["ffn1_w_down"][l])
        w = ins["w_in"][l]
        for half in range(2):
            for kind in range(3):
                tiles(w, 16 + 4 * kind + 2 * half, 2)
            tiles(w, 8 * half, 8)
            tiles(w, 28 + 2 * half, 2)
        tiles(ins["w_out"][l], 0, 8)
        ffn(ins["ffn2_w_gate"][l], 0, ins["ffn2_w_up"][l], 0, ins["ffn2_w_down"][l])
    w = ins["w_in_2"]

    def bcx(g):
        tiles(w, 48 + g, 1)
        tiles(w, 52 + g, 1)
        tiles(w, 32 + 4 * g, 4)

    bcx(0)
    for g in range(4):
        tiles(w, 16 + 4 * g, 4)
        if g:
            tiles(ins["w_out_ssm_2"][g - 1], 0, 8)
        if g < 3:
            bcx(g + 1)
    tiles(w, 0, 8)
    tiles(ins["w_out_ssm_2"][3], 0, 8)
    for p in range(6):
        if p < 5:
            tiles(w, 56 + 2 * p, 2)
        if p:
            for m in ("lru_w_r_2", "lru_w_i_2"):
                out.append((ins[m][p - 1], 256))
        if p < 5:
            tiles(w, 66 + 2 * p, 2)
    tiles(w, 8, 8)
    tiles(ins["w_out_lru_2"], 0, 8)
    tiles(ins["w_out_2"], 0, 8)
    ffn(ins["w_ffn_in_2"], 0, ins["w_ffn_in_2"], NH, ins["w_ffn_out_2"])
    return out


def build_program(nc, ins, out):
    with ExitStack() as ctx:
        k = Kernel(nc, ins, out, ctx)
        k.build()
        assert len(k.unit_done) == len(k.units)
        block = ctx.enter_context(nc.Block())
        block.sync(k.S.run)
        block.gpsimd(k.G.run)
        block.scalar(k.A.run)
        block.vector(k.V.run)
        block.tensor(k.P.run)


def fill(table, width, parts):
    c = np.zeros((128, width), np.float32)
    for name, a in parts:
        o, w = table[name]
        c[:a.shape[0] if a.ndim else 128, o:o + w] = a
    return c


def consts():
    p = np.arange(128)
    lm = [(p[None, :] >> s == (p[:, None] >> s) + 1) & ((p[:, None] >> s) % 2 == 0) for s in range(7)]
    cst = fill(CONSTS, NCONST, (
        ("ident", np.eye(128)), ("ones", np.ones((128, 2))), ("bd64", p[:, None] // 64 == p[None, :] // 64),
        ("mask", np.where(np.arange(512)[None, :] >= p[:, None], 0.0, NEG)), ("lmask", np.concatenate(lm, axis=1))))
    sel = fill(SEL, NSEL, (
        ("row", p[:, None] % 32 == np.arange(32)[None, :]),
        ("pair", np.arange(256)[None, :] // 64 == p[:, None] % 32)))
    rot = np.zeros((128, 128))
    for m in range(128):
        rot[m + 32 if m % 64 < 32 else m - 32, m] = -1.0 if m % 64 < 32 else 1.0
    inv = np.float32(10000.0) ** (-np.arange(0, 64, 2, dtype=np.float32) / np.float32(64))
    ang = (np.arange(512, dtype=np.float32)[None, :] * inv[p % 32][:, None]).astype(np.float64)
    rope = fill(TABLES, NROPE, (("rot", rot), ("cos", np.cos(ang)), ("sin", np.sin(ang))))
    rel = np.arange(512)[None, :] - p[:, None]
    ret = np.stack([np.where(rel >= 0, np.exp(np.maximum(rel, 0) * np.log1p(-2.0 ** (-5.0 - h))), 0.0)
                    for h in range(4)]).astype(np.float32)
    return cst, sel, rope, ret


def small_columns(x):
    parts = [(n, x[n].reshape(-1, 128).T) for n in (
        "ffn1_norm", "mix_norm", "ffn2_norm", "final_norm", "m_out_norm", "r_out_norm", "g_out_norm", "g_conv",
        "norm1_w_2", "norm2_w_2", "norm_f_w_2", "b_branch_gate_2", "ssm_conv_w_2", "ssm_conv_b_2",
        "ssm_norm_w_2", "lru_conv_w_2", "lru_conv_b_2", "lru_b_r_2", "lru_b_i_2", "lru_lambda_2")]
    parts += [(n, x[n].T) for n in ("m_i_bias", "m_f_bias", "g_a_log", "g_dt_bias", "ssm_dt_bias_2", "ssm_a_log_2")]
    parts.append(("ssm_d_2", np.repeat(x["ssm_d_2"].reshape(-1), 64).reshape(-1, 128).T))
    parts.append(("eps", np.full((128, 1), EPS, np.float32)))
    return fill(COLS, NCOLS, parts)


def by_tiles(w):
    k, n = w.shape
    return w.reshape(k // 128, 128, n // 128, 128).transpose(2, 1, 0, 3).reshape(n // 128, 128, k)


def padded(w, parts):
    g = np.zeros((w.shape[0], 128), np.float32)
    for at, a, b in parts:
        g[:, at:at + b - a] = w[:, a:b]
    return by_tiles(g)[0]


def lay_out(x):
    both = lambda f: np.ascontiguousarray(np.stack([f(0), f(1)]))
    a = {n: both(lambda l: by_tiles(x[n][l])) for n in (
        "ffn1_w_gate", "ffn1_w_up", "ffn1_w_down", "w_out", "ffn2_w_gate", "ffn2_w_up", "ffn2_w_down")}
    w = x["w_in"]
    a["w_in"] = both(lambda l: np.concatenate(
        [by_tiles(w[l][:, 0:1024]), by_tiles(w[l][:, 1032:2056]), by_tiles(w[l][:, 2056:4104])]))
    a["gate_w"] = both(lambda l: padded(w[l], ((0, 1024, 1028), (32, 1028, 1032), (64, 4104, 4108),
                                               (96, 4108, 4112))))
    w = x["w_in_2"][0]
    a["w_in_2"] = np.concatenate([by_tiles(w[:, 0:7168]), by_tiles(w[:, 7200:9760])])
    a["dt_w"] = padded(w, ((0, 7168, 7200),))
    for n in ("w_out_lru_2", "w_out_2", "w_ffn_in_2", "w_ffn_out_2"):
        a[n] = np.ascontiguousarray(by_tiles(x[n][0]))
    a["w_out_ssm_2"] = np.stack([by_tiles(x["w_out_ssm_2"][0][512 * g:512 * g + 512]) for g in range(4)])
    for n in ("lru_w_r_2", "lru_w_i_2"):
        a[n] = np.ascontiguousarray(x[n][0].reshape(5, 2, 128, 128).transpose(0, 2, 1, 3).reshape(5, 128, 256))
    a["x"] = x["x"][0]
    a["consts"], a["sel"], a["rope"], a["ret"] = consts()
    a["cols"] = small_columns(x)
    return a


def kernel(**inputs):
    import concourse.bacc as bacc
    from concourse.bass_utils import run_bass_kernel_spmd

    arrays = lay_out({k: np.ascontiguousarray(v) for k, v in inputs.items()})
    nc = bacc.Bacc("TRN2", target_bir_lowering=False, num_devices=1)
    ins = {k: nc.dram_tensor(f"in_{k}", a.shape, F, kind="ExternalInput").ap() for k, a in arrays.items()}
    out = nc.dram_tensor("out_0", (T, D), F, kind="ExternalOutput").ap()
    build_program(nc, ins, out)
    r = run_bass_kernel_spmd(nc, [{f"in_{k}": a for k, a in arrays.items()}], core_ids=[0])
    return r.results[0]["out_0"].reshape(1, T, D)
```

```python
import numpy as np
from contextlib import ExitStack

import concourse.bass as bass
from concourse import mybir

F = mybir.dt.float32
R = mybir.dt.float32r
ACT = mybir.ActivationFunctionType
ALU = mybir.AluOpType

T = 512
D = 1024
NH = 22
EPS = 1e-6
NEG = -3.0e38
OFF = (0, 512, 896, 1152)
QW = 1280
DIAG = (384, 0, 128, 256)
REST = (512, 896, 1152)
PIECES = (((0, 384, 512),), ((128, 0, 128), (256, 896, 256)), ((256, 128, 128), (384, 1152, 128)), ((384, 256, 128),))
NRAW = 4
NSPL = 4
SSM_PACE = 0.5
PACE = (0.4, 0.9, 0.7, 1.3, 0.7)

CONSTS, SEL, TABLES, COLS = {}, {}, {}, {}


def number(table, widths):
    at = 0
    for name, width in widths:
        table[name] = (at, width)
        at += width
    return at


NCONST = number(CONSTS, (("ident", 128), ("ones", 2), ("bd64", 128), ("mask", 512), ("lmask", 7 * 128)))
NSEL = number(SEL, (("row", 32), ("pair", 256)))
NROPE = number(TABLES, (("rot", 128), ("cos", 512), ("sin", 512)))
NCOLS = number(COLS, (
    ("ffn1_norm", 16), ("mix_norm", 16), ("ffn2_norm", 16), ("final_norm", 8),
    ("m_out_norm", 4), ("r_out_norm", 4), ("g_out_norm", 8), ("g_conv", 96),
    ("m_i_bias", 2), ("m_f_bias", 2), ("g_a_log", 2), ("g_dt_bias", 2),
    ("norm1_w_2", 8), ("norm2_w_2", 8), ("norm_f_w_2", 8), ("b_branch_gate_2", 16),
    ("ssm_conv_w_2", 96), ("ssm_conv_b_2", 24), ("ssm_dt_bias_2", 1), ("ssm_a_log_2", 1),
    ("ssm_d_2", 16), ("ssm_norm_w_2", 16), ("lru_conv_w_2", 40), ("lru_conv_b_2", 10),
    ("lru_b_r_2", 10), ("lru_b_i_2", 10), ("lru_lambda_2", 10), ("eps", 1)))
NSMALL = 392

TMP = (45, 46, 47, 48)
RSTD = 49
M_Y, M_G, M_BETA, M_HEAD = 0, 8, 9, (10, 21)
M_Q, M_K, M_V, M_D, M_NG, M_EM = 32, 34, 36, 40, 43, 44
M_ROWS = 32
S_ACC, S_CS, S_X, S_Z, S_XP, S_B, S_C, S_CB, S_D, S_SQ = 0, 8, (9, 17), (13, 21), 25, 33, 34, 35, (38, 41), 44
L_Y, L_U, L_YL, L_UH, L_R, L_I = 9, (29, 31), (33, 35), 37, 41, 43

L_GATE = ((29, 30, 33, 34), (31, 32, 35, 36))

B_PROJ, B_MISC, B_ATT, B_SSM, B_SUM = (0, 1), (2, 3, 4), 5, 6, 7


def drain(steps):
    while True:
        try:
            next(steps)
        except StopIteration as end:
            return end.value


class Engine:

    def __init__(self, sem):
        self.sem, self.n, self.todo, self.waited = sem, 0, [], {}

    def wait(self, *marks):
        for sem, value in marks:
            if self.waited.get(id(sem), 0) >= value:
                continue
            self.waited[id(sem)] = value
            self.todo.append(lambda e, sem=sem, value=value: e.wait_ge(sem, value))

    def put(self, make):
        self.todo.append(make)

    def mark(self, make):
        self.n += 1
        self.todo.append(lambda e: make(e).then_inc(self.sem, 1))
        return (self.sem, self.n)

    def here(self):
        return (self.sem, self.n)

    def run(self, e):
        for f in self.todo:
            f(e)


class Scalar(Engine):
    def act(self, out, in_, fn, **kw):
        return self.mark(lambda e: e.activation(out, in_, fn, **kw))

    def copy(self, out, in_, **kw):
        return self.act(out, in_, ACT.Copy, **kw)


class Vector(Engine):
    def tt(self, out, a, b, op):
        return self.mark(lambda e: e.tensor_tensor(out, a, b, op))

    def stt(self, out, a, s, b, op0, op1):
        return self.mark(lambda e: e.scalar_tensor_tensor(out=out, in0=a, scalar=s, in1=b, op0=op0, op1=op1))

    def ts(self, out, a, s1, op0, s2=None, op1=None):
        if op1 is None:
            return self.mark(lambda e: e.tensor_scalar(out, a, s1, None, op0))
        return self.mark(lambda e: e.tensor_scalar(out, a, s1, s2, op0, op1))

    def scan(self, out, d0, d1, op0, op1):
        return self.mark(lambda e: e.tensor_tensor_scan(out, d0, d1, 0.0, op0, op1))

    def recip(self, t):
        return self.mark(lambda e: e.reciprocal(t, t))

    def copy(self, out, in_):
        return self.mark(lambda e: e.tensor_copy(out, in_))

    def own(self):
        self.wait(self.here())


class Tensor(Engine):
    def mm(self, out, lhsT, rhs, start, stop):
        self.put(lambda e: e.matmul(out, lhsT, rhs, start=start, stop=stop))

    def mm_mark(self, out, lhsT, rhs, start, stop):
        return self.mark(lambda e: e.matmul(out, lhsT, rhs, start=start, stop=stop))

    def mm_share(self, out, lhsT, rhs, start, stop, last):
        make = lambda e: e.matmul(out, lhsT, rhs, start=start, stop=stop, skip_group_check=True)
        return self.mark(make) if last else self.put(make)

    def mm3(self, out, a, b, start, stop, last):
        (ah, al), (bh, bl) = a, b
        self.mm(out, ah, bh, start, False)
        self.mm(out, ah, bl, False, False)
        if last:
            return self.mm_mark(out, al, bh, False, stop)
        return self.mm(out, al, bh, False, stop)

    def turn(self, out, in_, ident):
        self.put(lambda e: e.transpose(out, in_, ident))

    def turn_mark(self, out, in_, ident):
        return self.mark(lambda e: e.transpose(out, in_, ident))


class Kernel:
    def __init__(self, nc, ins, out, ctx):
        self.nc, self.I, self.out = nc, ins, out
        self.units = plan_units(ins)
        sem = lambda n: ctx.enter_context(nc.semaphore(n))
        self.P, self.A, self.V = Tensor(sem("s_pe")), Scalar(sem("s_act")), Vector(sem("s_dve"))
        self.G, self.S = Engine(sem("s_pool")), Engine(sem("s_sp"))
        self.s_raw = [sem(f"s_raw{i}") for i in range(NRAW)]
        self.s_load = {n: sem(f"s_{n}") for n in ("x0", "x1", "x2", "x3", "cst", "sel", "col", "rope",
                                                  "ret0", "ret1")}
        self.n_load = {n: 0 for n in self.s_load}
        self.s_out = sem("s_out")
        self.at = -(-nc.sbuf_base // 64) * 64

        def place(name, width, dt=F):
            t = nc.alloc_sbuf_tensor_at(name, [128, width], dt, offset=self.at)
            self.at += -(-width * 4 // 64) * 64
            return t

        self.h = [place(f"h{i}", T) for i in range(8)]
        self.hn = [(place(f"hnh{i}", T, R), place(f"hnl{i}", T, R)) for i in range(8)]
        self.raw = [place(f"raw{i}", 1024) for i in range(NRAW)]
        self.spl = [(place(f"wh{i}", 1024, R), place(f"wl{i}", 1024, R)) for i in range(NSPL)]
        self.cst = place("cst", NCONST)
        self.selr = place("selr", NSEL, R)
        self.col = place("col", NCOLS)
        self.small = place("small", NSMALL)
        self.n_small = 0
        self.base = self.at
        assert self.base + 50 * 2048 <= nc.sbuf_usable_end, (nc.sbuf_usable_end - self.base) / 2048
        self.placed = {}
        self.ps = [ctx.enter_context(nc.psum_tensor(f"ps{i}", [128, T], F)) for i in range(8)]
        self.bank_read = [[] for _ in range(8)]
        self.tmp_read = [[] for _ in range(4)]
        self.n_proj = self.n_misc = self.n_tmp = 0
        self.h_ready = [[] for _ in range(8)]
        self.hn_ready = [[] for _ in range(8)]
        self.split_done, self.unit_done = [], []
        self.work, self.pace, self.due = [], 0.0, 0.0
        self.late = None
        self.taps = []
        self.ring = B_MISC

    def at_slot(self, i, n=1, dt=F):
        key = (i, n, "r" if dt == R else "f")
        if key not in self.placed:
            self.placed[key] = self.nc.alloc_sbuf_tensor_at(
                f"m{key[2]}{i}_{n}", [128, 512 * n], dt, offset=self.base + 2048 * i)
        return self.placed[key]

    def columns_for(self, n):
        self.n_small += n
        assert self.n_small <= NSMALL
        return self.small[:, self.n_small - n:self.n_small]

    def c(self, name, a=0, b=None, rows=128):
        o, w = CONSTS[name]
        return self.cst[0:rows, o + a:o + (w if b is None else b)]

    def cl(self, name, i=0, n=1, rows=128):
        o, _ = COLS[name]
        return self.col[0:rows, o + i:o + i + n]

    def next_tmp(self):
        self.n_tmp += 1
        k = self.n_tmp % 4
        return k, self.at_slot(TMP[k])

    def next_misc(self):
        self.n_misc += 1
        return self.ring[self.n_misc % len(self.ring)]

    def load(self, name, dst, src, queue=None):
        self.n_load[name] += 16
        (queue or self.G).put(lambda e: e.dma_start(dst, src).then_inc(self.s_load[name], 16))
        return (self.s_load[name], self.n_load[name])

    def fence(self):
        self.end_taps()
        ends = (self.P.here(), self.A.here(), self.V.here())
        for q in (self.A, self.V, self.G):
            q.wait(*ends)

    def step(self):
        g = self.work.pop(0)
        if next(g, "end") != "end":
            self.work.append(g)

    def beside(self, n=1):
        if self.taps:
            self.taps.pop(0)()
        self.due += n * self.pace
        while self.due >= 1.0:
            self.due -= 1.0
            if self.work:
                self.step()

    def end_taps(self):
        while self.taps:
            self.taps.pop(0)()

    def finish(self):
        self.end_taps()
        while self.work:
            self.step()

    def until(self, *those):
        while any(g in self.work for g in those):
            self.step()

    def fetch(self, u):
        src, n = self.units[u]
        raw = self.raw[u % NRAW]
        if u >= NRAW:
            self.S.wait(*self.split_done[u - NRAW])
        self.S.put(lambda e: e.dma_start(raw[:, 0:n], src).then_inc(self.s_raw[u % NRAW], 16))

    def split(self, u):
        _, n = self.units[u]
        raw, (hi, lo) = self.raw[u % NRAW], self.spl[u % NSPL]
        landed = (self.s_raw[u % NRAW], 16 * (u // NRAW + 1))
        self.A.wait(landed)
        if u >= NSPL:
            self.A.wait(self.unit_done[u - NSPL])
        high = self.A.copy(hi[:, 0:n], raw[:, 0:n])
        self.V.wait(landed, high)
        if u >= NSPL:
            self.V.wait(self.unit_done[u - NSPL])
        low = self.V.tt(lo[:, 0:n], raw[:, 0:n], hi[:, 0:n].bitcast(F), ALU.subtract)
        self.split_done.append((high, low))
        if u + NRAW < len(self.units):
            self.fetch(u + NRAW)

    def unit(self):
        u = len(self.unit_done)
        hi, lo = self.spl[u % NSPL]
        n = self.units[u][1]
        self.P.wait(*self.split_done[u])
        v = lambda t: t[:, 0:n].rearrange("p (k c) -> p k c", c=128)
        return v(hi), v(lo)

    def unit_used(self, done):
        self.unit_done.append(done)
        u = len(self.split_done)
        if u < len(self.units):
            self.split(u)

    def product(self, bank, xs, ready):
        self.P.wait(*self.bank_read[bank])
        nk = len(xs)
        for k0 in range(0, nk, 8):
            wh, wl = self.unit()
            kn = min(8, nk - k0)
            for k in range(kn):
                if k % 2 == 0:
                    self.beside()
                self.P.wait(*ready[k0 + k])
                done = self.P.mm3(self.ps[bank][:, :], (wh[:, k, :], wl[:, k, :]),
                                  (xs[k0 + k][0][:, :], xs[k0 + k][1][:, :]),
                                  k0 + k == 0, k0 + k == nk - 1, k == kn - 1)
            self.unit_used(done)
        return done

    def proj(self, n, xs, ready, take):
        for i in range(n):
            bank = B_PROJ[self.n_proj % 2]
            self.n_proj += 1
            done = self.product(bank, xs, ready)
            self.run_late()
            self.bank_read[bank] = take(i, self.ps[bank], done)

    def proj_h(self, n, take):
        self.proj(n, self.hn, self.hn_ready, take)

    def proj_tokens(self, take):
        bank = B_PROJ[self.n_proj % 2]
        self.n_proj += 1
        self.P.wait(*self.bank_read[bank])
        wh, wl = self.unit()
        for j in range(4):
            js = slice(128 * j, 128 * j + 128)
            for k in range(8):
                self.P.wait(*self.hn_ready[k])
                done = self.P.mm3(self.ps[bank][:, js], (self.hn[k][0][:, js], self.hn[k][1][:, js]),
                                  (wh[:, k, :], wl[:, k, :]), k == 0, k == 7, j == 3 and k == 7)
        self.unit_used(done)
        self.bank_read[bank] = take(self.ps[bank], done)
        self.beside(4)

    def split_tile(self, src, hi, lo, ready):
        self.A.wait(ready)
        high = self.A.copy(hi, src)
        self.V.wait(high, ready)
        low = self.V.tt(lo, src, hi.bitcast(F), ALU.subtract)
        return [high, low]

    def h_new(self, i, done, gain):
        self.h_ready[i] = [done]
        kx, x = self.next_tmp()
        self.V.wait(*self.tmp_read[kx], done)
        scaled = self.V.ts(x[:, :], self.h[i][:, :], self.cl(gain[0], gain[1] + i), ALU.mult)
        hi, lo = self.hn[i]
        self.A.wait(self.hn_last)
        self.V.wait(self.hn_last)
        self.hn_ready[i] = self.split_tile(x[:, :], hi[:, :], lo[:, :], scaled)
        self.tmp_read[kx] = self.hn_ready[i]
        ks, sq = self.next_tmp()
        self.A.wait(*self.tmp_read[ks], done)
        squared = self.A.act(sq[:, :], self.h[i][:, :], ACT.Square)

        def later():
            self.rs_ready = None
            self.P.wait(squared, *self.bank_read[B_SUM])
            for j in range(4):
                m = self.P.mm_share(self.ps[B_SUM][:, j:j + 1], sq[:, 128 * j:128 * j + 128],
                                    self.c("ones", 0, 1), i == 0 and j == 0, i == 7, j == 3)
            self.tmp_read[ks] = [m]
            self.sum_done = m
            if i == 7:
                self.h_rstd()

        self.late = later

    def rstd_columns(self, bank, cols, n, done, eps=EPS):
        self.A.wait(done, *self.col_read)
        root = self.A.act(cols, bank[:, 0:4], ACT.Sqrt, bias=self.cl("eps"), scale=1.0 / n)
        self.V.wait(root)
        return root, self.V.recip(cols)

    def rows_of(self, out, cols, ready):
        self.P.wait(ready)
        for j in range(4):
            put = self.P.mm_mark if j == 3 else self.P.mm
            m = put(out[:, 128 * j:128 * j + 128], cols[:, j:j + 1].to_broadcast([128, 128]),
                    self.c("ident"), True, True)
        return m

    def h_rstd(self):
        root, cols = self.rstd_columns(self.ps[B_SUM], self.rc, D, self.sum_done)
        self.bank_read[B_SUM] = [root]
        b = self.next_misc()
        self.P.wait(*self.bank_read[b])
        spread = self.rows_of(self.ps[b], self.rc, cols)
        self.V.wait(spread)
        self.rs_ready = self.V.copy(self.rs[:, :], self.ps[b][:, :])
        self.bank_read[b] = [self.rs_ready]
        self.rc_ready = cols

    def run_late(self):
        if self.late:
            self.late()
            self.late = None
            if self.rs_ready:
                self.V.wait(self.rs_ready)

    def norm_ready(self):
        self.run_late()
        self.V.wait(self.rs_ready)

    def add_h(self, scale, gain):
        def take(i, bank, done):
            self.V.wait(done, *self.h_ready[i])
            m = self.V.stt(self.h[i][:, :], bank[:, :], scale, self.h[i][:, :], ALU.mult, ALU.add)
            self.h_new(i, m, gain)
            return [m]
        return take

    def ffn(self, scale, gain):
        self.fence()
        hid = [(self.at_slot(2 * i, dt=R), self.at_slot(2 * i + 1, dt=R)) for i in range(NH)]
        ready = [[] for _ in range(NH)]
        held = []

        def gate(i, bank, done):
            k, g = self.next_tmp()
            self.V.wait(done, *self.tmp_read[k])
            m = self.V.tt(g[:, :], bank[:, :], self.rs[:, :], ALU.mult)
            self.A.wait(m)
            held.append((k, g, self.A.act(g[:, :], g[:, :], ACT.Silu)))
            return [m]

        def up(i, bank, done):
            k, g, silu = held.pop()
            self.V.wait(silu, done)
            m = self.V.tt(g[:, :], g[:, :], self.rs[:, :], ALU.mult)
            self.V.wait(m)
            both = self.V.tt(g[:, :], g[:, :], bank[:, :], ALU.mult)
            ready[i] = self.split_tile(g[:, :], hid[i][0][:, :], hid[i][1][:, :], both)
            self.tmp_read[k] = ready[i]
            return [both]

        for i in range(NH):
            self.proj_h(1, gate)
            self.proj_h(1, lambda _, b, d, i=i: up(i, b, d))
        self.hn_last = self.P.here()
        self.proj(8, hid, ready, self.add_h(scale, gain))

    def softplus(self, out, x, t1, t2, t3, ready):
        A, V = self.A, self.V
        A.wait(ready)
        a = A.act(t1, x, ACT.Abs)
        A.wait(a)
        e = A.act(t1, t1, ACT.Exp, scale=-1.0)
        V.wait(e)
        u = V.ts(t2, t1, 1.0, ALU.add)
        A.wait(u)
        ln = A.act(t3, t2, ACT.Ln)
        V.wait(u)
        m = V.stt(t1, t2, -1.0, t1, ALU.add, ALU.subtract)
        yield
        V.wait(ln, m)
        V.recip(t2)
        V.own()
        V.tt(t1, t1, t2, ALU.mult)
        V.own()
        V.tt(t3, t3, t1, ALU.subtract)
        V.own()
        return V.stt(out, x, 0.0, t3, ALU.max, ALU.add)

    def split_rows(self, dst, rows, n, ready):
        self.A.wait(ready)
        if n < 32:
            self.G.wait(ready)
            z = self.G.mark(lambda e: e.memset(dst[0:64, :].bitcast(F), 0.0))
            self.A.wait(z)
            self.V.wait(z)
        hi = self.A.copy(dst[0:n, :], rows)
        self.V.wait(hi, ready)
        return self.V.tt(dst[32:32 + n, :], rows, dst[0:n, :].bitcast(F), ALU.subtract)

    def spread(self, rows, h, ready):
        b = self.next_misc()
        self.P.wait(ready, *self.bank_read[b])
        return b, self.P.mm_mark(self.ps[b][:, :], self.selr[0:64, h:h + 1].to_broadcast([64, 128]),
                                 rows[0:64, :], True, True)

    def spread_pair(self, rows, h, ready):
        b = self.next_misc()
        self.P.wait(ready, *self.bank_read[b])
        return b, self.P.mm_mark(self.ps[b][:, :], self.selr[0:64, 32 + 64 * h:160 + 64 * h],
                                 rows[0:64, :], True, True)

    def columns(self, dst, rows, n, ready):
        b = self.next_misc()
        self.P.wait(ready, *self.bank_read[b])
        for j in range(4):
            turn = self.P.turn_mark if j == 3 else self.P.turn
            t = turn(self.ps[b][:, n * j:n * j + n], rows[:, 128 * j:128 * j + 128], self.c("ident", 0, n, rows=n))
        self.V.wait(t)
        m = self.V.copy(dst, self.ps[b][:, 0:4 * n])
        self.bank_read[b] = [m]
        return m

    def decay(self, b, spread, col, out):
        self.V.wait(spread)
        for jt in range(4):
            w = T - 128 * jt
            m = self.V.stt(out[:, OFF[jt]:OFF[jt] + w], self.ps[b][:, 128 * jt:T], col(jt), self.c("mask", 0, w),
                           ALU.subtract, ALU.min)
        self.bank_read[b] = [m]
        self.A.wait(m)
        return self.A.act(out[:, 0:QW], out[:, 0:QW], ACT.Exp)

    def turn_tile(self, src, ready):
        b = self.next_misc()
        self.P.wait(*ready, *self.bank_read[b])
        for j in range(4):
            js = slice(128 * j, 128 * j + 128)
            turn = self.P.turn_mark if j == 3 else self.P.turn
            t = turn(self.ps[b][:, js], src[:, js], self.c("ident"))
        return b, t

    def keep(self, dst, got, scale=None, fn=None):
        def take(i, bank, done):
            d = dst(i)
            self.V.wait(done)
            if scale is None:
                m = self.V.tt(d[:, :], bank[:, :], self.rs[:, :], ALU.mult)
            else:
                m = self.V.stt(d[:, :], bank[:, :], scale, self.rs[:, :], ALU.mult, ALU.mult)
            got[i] = m
            if fn is not None:
                self.A.wait(m)
                got[i] = fn(d, i)
            return [m]
        return take

    def conv(self, dst, got, w, bias=None, fn=None):
        def take(i, bank, done):
            self.end_taps()
            k0, x = self.next_tmp()
            s = dst(i)
            self.V.wait(done, *self.tmp_read[k0])
            m = self.V.tt(x[:, :], bank[:, :], self.rs[:, :], ALU.mult)

            def first():
                self.A.wait(m)
                if bias is None:
                    a = self.A.copy(s[:, :], x[:, :], scale=w(i, 3))
                else:
                    a = self.A.act(s[:, :], x[:, :], ACT.Identity, scale=w(i, 3), bias=bias(i))
                self.V.wait(a)
                tap(2)

            def tap(k):
                d = 3 - k
                self.V.own()
                return self.V.stt(s[:, d:T], x[:, 0:T - d], w(i, k), s[:, d:T], ALU.mult, ALU.add)

            def last():
                c = tap(0)
                self.tmp_read[k0] = [c]
                got[i] = c
                if fn is not None:
                    got[i] = fn(s, c)

            self.taps = [first, lambda: tap(1), last]
            return [m]
        return take

    def silu(self, x, ready):
        self.A.wait(ready)
        return self.A.act(x[:, :], x[:, :], ACT.Silu)

    def gated_norm(self, o, ready, gain, y, gate, b, spread):
        self.V.wait(ready, spread)
        m = self.V.stt(o[:, :], o[:, :], gain, self.ps[b][:, :], ALU.mult, ALU.mult)
        self.bank_read[b] = [m]
        self.V.wait(gate, m)
        return self.V.tt(y[:, :], o[:, :], y[:, :], ALU.mult)

    def half_norm(self, o, ready, gain, y, gate, sq):
        A, V, P = self.A, self.V, self.P
        A.wait(ready)
        s = A.act(sq[:, :], o[:, :], ACT.Square)
        yield
        b = self.next_misc()
        P.wait(s, *self.bank_read[b])
        m = P.mm_mark(self.ps[b][:, :], self.c("bd64"), sq[:, :], True, True)
        A.wait(m)
        root = A.act(sq[:, :], self.ps[b][:, :], ACT.Sqrt, bias=self.cl("eps"), scale=1.0 / 64)
        self.bank_read[b] = [root]
        yield
        V.wait(root)
        r = V.recip(sq[:, :])
        V.wait(r, ready)
        m = V.stt(o[:, :], o[:, :], gain, sq[:, :], ALU.mult, ALU.mult)
        V.wait(gate, m)
        return V.tt(y[:, :], o[:, :], y[:, :], ALU.mult)

    def small_product(self):
        self.small_done = self.product(B_ATT, self.hn, self.hn_ready)
        self.norm_ready()

    def rows(self, l):
        P, A, V = self.P, self.A, self.V
        rows = [self.at_slot(M_ROWS + q) for q in range(4)]
        ri, rf, ra, rb = (r[0:4, :] for r in rows)
        t1, t2, t3, t4 = (self.at_slot(M_ROWS + 4 + q)[0:4, :] for q in range(4))
        V.wait(self.small_done)
        for q, r in enumerate((ri, rf, ra, rb)):
            got = V.tt(r, self.ps[B_ATT][32 * q:32 * q + 4, :], self.rs[32 * q:32 * q + 4, :], ALU.mult)
        self.bank_read[B_ATT] = [got]
        V.own()
        a = V.ts(ra, ra, self.cl("g_dt_bias", l, rows=4), ALU.add)
        sp = yield from self.softplus(ra, ra, t1, t2, t4, a)
        A.wait(sp)
        ea = A.act(self.one_col[0:4, :], self.cl("g_a_log", l, rows=4), ACT.Exp)
        one = lambda n: self.c("ones", 0, 1, rows=4).to_broadcast([4, n])
        V.wait(ea, sp)
        la = V.ts(ra, ra, self.one_col[0:4, :], ALU.mult, -1.0, ALU.mult)
        V.wait(la)
        for j in range(4):
            js = slice(128 * j, 128 * j + 128)
            g = V.scan(t2[:, js], one(128), ra[:, js], ALU.mult, ALU.add)
        yield
        yield
        self.g_ready = self.split_rows(self.at_slot(M_G, dt=R), t2, 4, g)
        self.g_cols_ready = self.columns(self.g_cols, t2, 4, g)
        yield
        A.wait(got)
        beta = A.act(rb, rb, ACT.Sigmoid)
        self.b_ready = self.split_rows(self.at_slot(M_BETA, dt=R), rb, 4, beta)
        yield
        self.b_cols_ready = self.columns(self.b_cols, rb, 4, beta)
        self.delta_rows = True
        yield
        V.ts(ri, ri, self.cl("m_i_bias", l, rows=4), ALU.add)
        f = V.ts(rf, rf, self.cl("m_f_bias", l, rows=4), ALU.add, -1.0, ALU.mult)
        V.wait(self.g_ready, self.g_cols_ready)
        A.wait(self.g_ready, self.g_cols_ready)
        f = yield from self.softplus(rf, rf, t1, t2, t3, f)
        V.wait(f)
        V.scan(t2, one(512), rf, ALU.mult, ALU.subtract)
        V.own()
        na = V.tt(rf, t2, ri, ALU.subtract)
        yield
        self.a_cols_ready = self.columns(self.m_cols, rf, 4, na)
        V.wait(na)
        a = V.ts(ri, rf, -1.0, ALU.mult)
        V.wait(a)
        V.scan(t3, ri, self.c("mask", 4, 5, rows=4).to_broadcast([4, 512]), ALU.max, ALU.add)
        V.own()
        m = V.tt(t2, t2, t3, ALU.add)
        A.wait(m)
        em = A.act(t2, t2, ACT.Exp, scale=-1.0)
        yield
        ng = V.ts(t3, t3, -1.0, ALU.mult)
        self.em_ready = self.split_rows(self.at_slot(M_EM, dt=R), t2, 4, em)
        self.ng_ready = self.split_rows(self.at_slot(M_NG, dt=R), t3, 4, ng)
        self.rows_end = [P.here(), A.here(), V.here()]

    def mixer(self, l, gain):
        P, A, V = self.P, self.A, self.V
        self.fence()
        self.small_product()
        y = [self.at_slot(M_Y + i) for i in range(8)]
        y_ready = [None] * 8
        self.ring = (*B_MISC, B_SSM, B_SUM)
        self.gate_ready = {}
        self.delta_rows = False
        self.heads_end = []
        heads = [self.delta(l, h, h % 2, y, y_ready) for h in range(4)]
        rows = self.rows(l)
        self.pace = PACE[0]
        self.work.append(rows)
        self.delta_qkv(l, 0)
        self.pace = PACE[4]
        self.work += heads[0:2]
        self.gates(y, 0, ACT.Sigmoid)
        self.gates(y, 4, ACT.Silu)
        self.until(rows)
        self.pace = PACE[1]
        q, k, v = self.qkv()
        mlstm = self.mlstm(l, q, k, v, y, y_ready)
        self.work.append(mlstm)
        self.until(*heads[0:2])
        for e in (A, V):
            e.wait(*self.heads_end)
        self.pace = PACE[2]
        self.delta_qkv(l, 2)
        self.work += heads[2:4]
        self.until(mlstm)
        self.pace = PACE[3]
        q, k, v = self.qkv(rope=True)
        retention = self.retention(l, q, k, v, y, y_ready)
        self.work.append(retention)
        self.gates(y, 2, ACT.Silu)
        self.gates(y, 6, ACT.Silu)
        self.hn_last = P.here()
        self.until(retention)
        places = [(M_Q + 2 * i, M_Q + 2 * i + 1) for i in range(6)] + [(M_G, M_BETA), (M_EM, M_HEAD[0])]
        parts = [(self.at_slot(a, dt=R), self.at_slot(b, dt=R)) for a, b in places]
        split = [None] * 8

        def splits(those):
            for i in those:
                split[i] = self.split_tile(y[i][:, :], parts[i][0][:, :], parts[i][1][:, :], y_ready[i])
                yield

        for e in (A, V):
            e.wait(*self.retention_end)
        self.work.append(splits(range(6)))
        self.finish()
        for e in (A, V):
            e.wait(*self.heads_end)
        drain(splits((6, 7)))
        self.pace = 0.0
        self.ring = B_MISC
        self.proj(8, parts, split, self.add_h(1.0, gain))

    def gates(self, y, i0, fn):
        def after(d, i):
            m = self.A.act(d[:, :], d[:, :], fn)
            self.gate_ready[i0 + i] = m
            return m
        self.proj_h(2, self.keep(lambda i: y[i0 + i], {}, fn=after))

    def qkv(self, rope=False):
        P, A, V, G = self.P, self.A, self.V, self.G
        q, k = [self.at_slot(M_Q + i) for i in range(2)], [self.at_slot(M_K + i) for i in range(2)]
        v = [self.at_slot(M_V + i) for i in range(4)]
        for e in (V, G, A):
            e.wait(*self.rows_end)
        qm, km, vm = {}, {}, {}
        if rope:
            tab = self.at_slot(M_D, 3)
            tab_ready = self.load("rope", tab[:, 0:NROPE], self.I["rope"])
        for j in range(4):
            zero = G.mark(lambda e, j=j: e.memset(v[j][:, :], 0.0 if rope else 1.0))
        self.proj_h(2, self.keep(lambda i: q[i], qm))
        self.proj_h(2, self.keep(lambda i: k[i], km, scale=0.125))
        for n in range(2):
            def take(bank, done):
                V.wait(done, zero, self.rc_ready)
                for j in range(4):
                    for s in range(2):
                        o = 256 * n + 128 * s + 64 * s
                        m = V.ts(v[j][:, o:o + 64], bank[:, 128 * j + 64 * s:128 * j + 64 * s + 64],
                                 self.rc[:, j:j + 1], ALU.mult)
                vm[n] = m
                return [m]
            self.proj_tokens(take)
        if rope:
            tb = lambda n: tab[:, TABLES[n][0]:TABLES[n][0] + TABLES[n][1]]
            for ready, x in ((qm, q), (km, k)):
                for i in range(2):
                    b = self.next_misc()
                    P.wait(ready[i], tab_ready, *self.bank_read[b])
                    m = P.mm_mark(self.ps[b][:, :], tb("rot"), x[i][:, :], True, True)
                    kt, r = self.next_tmp()
                    V.wait(m, tab_ready, *self.tmp_read[kt])
                    s = V.tt(r[:, :], self.ps[b][:, :], tb("sin"), ALU.mult)
                    self.bank_read[b] = [s]
                    V.tt(x[i][:, :], x[i][:, :], tb("cos"), ALU.mult)
                    V.own()
                    ready[i] = V.tt(x[i][:, :], x[i][:, :], r[:, :], ALU.add)
                    self.tmp_read[kt] = [ready[i]]
        return (q, qm), (k, km), (v, vm)

    def attend(self, h, q, k, v, weigh):
        P = self.P
        (qt, qm), (kt, km), (vt, vm) = q, k, v
        p, pr = h // 2, slice(64 * (h % 2), 64 * (h % 2) + 64)
        out = self.ps[B_ATT]
        got = []

        def score(jt):
            w = T - 128 * jt
            b = self.next_misc()
            P.wait(qm[p], km[p], *self.bank_read[b])
            m = P.mm_mark(self.ps[b][:, 0:w], kt[p][pr, 128 * jt:128 * jt + 128], qt[p][pr, 128 * jt:T], True, True)
            self.V.wait(m)
            got.append(weigh(jt, self.ps[b][:, 0:w], w))
            self.bank_read[b] = [got[-1][1]]

        def values(jt):
            place, m = got[jt]
            P.wait(m, vm[0], vm[1], *self.bank_read[B_ATT])
            return P.mm_mark(out[:, 128 * jt:T], vt[jt][:, 128 * h:128 * h + 128], place, jt == 0, jt == 3)

        score(0)
        score(1)
        yield
        score(2)
        score(3)
        values(0)
        values(1)
        yield
        values(2)
        return values(3)

    def mlstm(self, l, q, k, v, y, y_ready):
        P, A, V = self.P, self.A, self.V
        d = self.at_slot(M_D, 3)
        att = [P.here()]
        for p in range(2):
            o, den = self.at_slot(M_Q + p), self.at_slot(M_K + p)
            for s in range(2):
                h = 2 * p + s
                b, spread = self.spread(self.at_slot(M_NG, dt=R), h, self.ng_ready)
                V.wait(self.a_cols_ready, *att)
                w_ready = self.decay(b, spread, lambda jt: self.m_cols[:, 4 * jt + h:4 * jt + h + 1], d)
                yield
                V.wait(w_ready)

                def weigh(jt, scores, w):
                    place = d[:, OFF[jt]:OFF[jt] + w]
                    return place, V.tt(place, scores, place, ALU.mult)

                done = yield from self.attend(h, q, k, v, weigh)
                att = [done]
                num, dn = slice(64 * s, 64 * s + 64), slice(64 - 64 * s, 128 - 64 * s)
                A.wait(done)
                n = A.copy(o[num, :], self.ps[B_ATT][num, :])
                a = A.act(den[num, :], self.ps[B_ATT][dn, :], ACT.Abs)
                self.bank_read[B_ATT] = [a]
                yield
            b, spread = self.spread_pair(self.at_slot(M_EM, dt=R), 2 * p, self.em_ready)
            V.wait(a, spread)
            m = V.tt(den[:, :], den[:, :], self.ps[b][:, :], ALU.max)
            self.bank_read[b] = [m]
            V.own()
            V.recip(den[:, :])
            V.own()
            m = V.tt(o[:, :], o[:, :], den[:, :], ALU.mult)
            A.wait(m)
            yield
            y_ready[p] = yield from self.half_norm(o, m, self.cl("m_out_norm", 2 * l + p), y[p],
                                                   self.gate_ready[p], den)
            yield
        self.rows_end = [P.here(), A.here(), V.here()]

    def retention(self, l, q, k, v, y, y_ready):
        P, A, V, G = self.P, self.A, self.V, self.G
        d = self.at_slot(M_D, 3)
        att = [P.here(), V.here()]
        ret_read = [[P.here(), V.here()], [P.here(), V.here()]]
        for p in range(2):
            o = self.at_slot(M_Q + p)
            for s in range(2):
                h = 2 * p + s
                tab = self.at_slot((M_NG, M_EM)[s])
                G.wait(*ret_read[s])
                tab_ready = self.load(f"ret{s}", tab[:, :], self.I["ret"][h])
                V.wait(tab_ready, *att)

                def weigh(jt, scores, w):
                    place = d[:, OFF[jt]:OFF[jt] + w]
                    return place, V.tt(place, scores, tab[:, 0:w], ALU.mult)

                done = yield from self.attend(h, q, k, v, weigh)
                att = [done]
                ret_read[s] = [V.here()]
                num = slice(64 * s, 64 * s + 64)
                A.wait(done)
                m = A.copy(o[num, :], self.ps[B_ATT][num, :])
                self.bank_read[B_ATT] = [m]
                yield
            while 2 + p not in self.gate_ready:
                yield
            y_ready[2 + p] = yield from self.half_norm(o, m, self.cl("r_out_norm", 2 * l + p), y[2 + p],
                                                       self.gate_ready[2 + p], self.at_slot(M_K + p))
            yield
        self.retention_end = [P.here(), A.here(), V.here()]

    def delta_qkv(self, l, h0):
        self.qkv_ready = {}
        for kind in range(3):
            got = {}
            self.proj_h(2, self.conv(lambda i, kind=kind: self.at_slot(M_HEAD[i] + kind), got,
                                     lambda i, k, kind=kind: self.cl("g_conv", 48 * l + 12 * k + 4 * kind + h0 + i),
                                     fn=self.silu))
            self.qkv_ready[kind] = got
        self.end_taps()

    def delta(self, l, h, i, y, y_ready):
        P, A, V = self.P, self.A, self.V
        at = [self.at_slot(M_HEAD[i] + n) for n in range(11)]
        Q, K, vt, eg, et, kbT, vb, kd, kb, pt, Z = at
        X, am, St, o, Y, U, wt = K, vt, vt, et, kbT, kbT, kb
        four = [slice(128 * c, 128 * c + 128) for c in range(4)]
        blk = lambda t: t[:, :].rearrange("p (c n) -> p c n", c=4)
        of_head = lambda t: t.rearrange("p (c h) -> p h c", h=4)[:, h, :]
        wide = lambda t: t.unsqueeze(2).to_broadcast([128, 4, 128])
        sd = self.d_cols[i]
        q_ready, k_ready, v_ready = (self.qkv_ready[n][i] for n in range(3))
        ps = self.ps
        for x, sq, ready in ((Q, kd, q_ready), (K, kb, k_ready)):
            A.wait(ready)
            squared = A.act(sq[:, :], x[:, :], ACT.Square)
        yield
        b = self.next_misc()
        P.wait(squared, *self.bank_read[b])
        for n, sq in enumerate((kd, kb)):
            for c in range(4):
                put = P.mm_mark if n == 1 and c == 3 else P.mm
                m = put(ps[b][:, 4 * n + c:4 * n + c + 1], sq[:, four[c]], self.c("ones", 0, 1), True, True)
        A.wait(m)
        root = A.act(sd[:, 0:8], ps[b][:, 0:8], ACT.Sqrt, bias=self.cl("eps"))
        self.bank_read[b] = [root]
        V.wait(root)
        rms = V.recip(sd[:, 0:8])
        yield
        norm = []
        for n, (x, ready, s) in enumerate(((Q, q_ready, 128.0 ** -0.5), (K, k_ready, 1.0))):
            b = self.next_misc()
            P.wait(*self.bank_read[b])
            spread = self.rows_of(ps[b], sd[:, 4 * n:4 * n + 4], rms)
            V.wait(spread, ready)
            norm.append(V.stt(x[:, :], x[:, :], s, ps[b][:, :], ALU.mult, ALU.mult))
            self.bank_read[b] = [norm[-1]]
        q_ready, k_ready = norm
        while not self.delta_rows:
            yield
        yield
        b, t = self.turn_tile(vt, [v_ready])
        V.wait(t, self.b_cols_ready)
        vb_ready = V.tt(blk(vb), blk(ps[b]), wide(of_head(self.b_cols)), ALU.mult)
        self.bank_read[b] = [vb_ready]
        v_turned = t
        b, spread = self.spread(self.at_slot(M_G, dt=R), h, self.g_ready)
        A.wait(spread)
        eg_ready = A.act(eg[:, :], ps[b][:, :], ACT.Exp)
        V.wait(spread, eg_ready, self.g_cols_ready)
        for c in range(4):
            m = V.stt(et[:, four[c]], ps[b][:, four[c]], self.g_cols[:, 4 * c + h:4 * c + h + 1],
                      self.c("mask", 0, 128), ALU.subtract, ALU.min)
        A.wait(m)
        et_ready = A.act(et[:, :], et[:, :], ACT.Exp)
        last_g = V.tt(sd[:, 0:4], ps[b][:, 127::128], of_head(self.g_cols), ALU.subtract)
        self.bank_read[b] = [last_g]
        A.wait(last_g, self.g_cols_ready)
        kd_col = A.act(sd[:, 0:4], sd[:, 0:4], ACT.Exp)
        kb_col = A.act(sd[:, 4:8], of_head(self.g_cols), ACT.Exp)
        V.wait(kb_col)
        kb_col = V.tt(sd[:, 4:8], sd[:, 4:8], of_head(self.b_cols), ALU.mult)
        yield
        b, spread = self.spread(self.at_slot(M_BETA, dt=R), h, self.b_ready)
        V.wait(spread, k_ready)
        kbT_ready = V.tt(kbT[:, :], K[:, :], ps[b][:, :], ALU.mult)
        self.bank_read[b] = [kbT_ready]
        b, t = self.turn_tile(K, [k_ready])
        V.wait(t, kd_col, kb_col)
        kd_ready = V.tt(blk(kd), blk(ps[b]), wide(sd[:, 0:4]), ALU.mult)
        kb_ready = V.tt(blk(kb), blk(ps[b]), wide(sd[:, 4:8]), ALU.mult)
        self.bank_read[b] = [kb_ready]
        yield
        b = self.next_misc()
        P.wait(k_ready, q_ready, *self.bank_read[b])
        for c in range(4):
            put = P.mm_mark if c == 3 else P.mm
            m = put(ps[b][:, four[c]], K[:, four[c]], Q[:, four[c]], True, True)
        V.wait(m, et_ready)
        pt_ready = V.tt(pt[:, :], ps[b][:, :], et[:, :], ALU.mult)
        self.bank_read[b] = [pt_ready]
        b = self.next_misc()
        P.wait(kbT_ready, *self.bank_read[b])
        for c in range(4):
            put = P.mm_mark if c == 3 else P.mm
            k_read = put(ps[b][:, four[c]], K[:, four[c]], kbT[:, four[c]], True, True)
        V.wait(k_read)
        a_ready = V.tt(et[:, :], ps[b][:, :], et[:, :], ALU.mult)
        self.bank_read[b] = [a_ready]
        V.wait(eg_ready)
        qg_ready = V.tt(Q[:, :], Q[:, :], eg[:, :], ALU.mult)
        yield
        lm = lambda s: self.c("lmask", 128 * s, 128 * s + 128).unsqueeze(1).to_broadcast([128, 4, 128])
        V.wait(a_ready, v_turned)
        m = V.tt(blk(am), blk(et), lm(0), ALU.mult)
        V.wait(m)
        z_ready = V.tt(blk(Z), self.c("ident").unsqueeze(1).to_broadcast([128, 4, 128]), blk(am), ALU.subtract)
        b, t = self.turn_tile(Z, [z_ready])
        A.wait(t, k_read, k_ready)
        x_ready = A.copy(X[:, :], ps[b][:, :])
        self.bank_read[b] = [x_ready]
        V.wait(z_ready)
        am_ready = V.tt(blk(am), blk(et), lm(1), ALU.mult)
        y_read = k_read
        yield
        for s in range(1, 7):
            b = self.next_misc()
            P.wait(am_ready, x_ready, *self.bank_read[b])
            for c in range(4):
                put = P.mm_mark if c == 3 else P.mm
                am_read = put(ps[b][:, four[c]], am[:, four[c]], X[:, four[c]], True, True)
            A.wait(am_read, y_read)
            y_ready_ = A.copy(Y[:, :], ps[b][:, :])
            self.bank_read[b] = [y_ready_]
            yield
            if s < 6:
                V.wait(am_read)
                am_ready = V.tt(blk(am), blk(et), lm(s + 1), ALU.mult)
                b = self.next_misc()
                P.wait(y_ready_, z_ready, *self.bank_read[b])
                for c in range(4):
                    put = P.mm_mark if c == 3 else P.mm
                    m = put(ps[b][:, four[c]], Z[:, four[c]], Y[:, four[c]], True, True)
                V.wait(m, x_ready)
                x_ready = V.tt(X[:, :], X[:, :], ps[b][:, :], ALU.subtract)
                self.bank_read[b] = [x_ready]
            bz = self.next_misc()
            P.wait(y_ready_, z_ready, *self.bank_read[bz])
            for c in range(4):
                put = P.mm_mark if c == 3 else P.mm
                y_read = put(ps[bz][:, four[c]], Y[:, four[c]], Z[:, four[c]], True, True)
            V.wait(y_read, z_ready)
            z_ready = V.tt(Z[:, :], Z[:, :], ps[bz][:, :], ALU.subtract)
            self.bank_read[bz] = [z_ready]
            yield
        b = self.next_misc()
        P.wait(kb_ready, z_ready, *self.bank_read[b])
        for c in range(4):
            put = P.mm_mark if c == 3 else P.mm
            m = put(ps[b][:, four[c]], kb[:, four[c]], Z[:, four[c]], True, True)
        A.wait(m, kb_ready)
        wt_ready = A.copy(wt[:, :], ps[b][:, :], scale=-1.0)
        self.bank_read[b] = [wt_ready]
        yield
        s_ready = None
        for c in range(4):
            b = self.next_misc()
            P.wait(vb_ready, z_ready, *self.bank_read[b])
            if c == 0:
                m = P.mm_mark(ps[b][:, 0:128], Z[:, four[c]], vb[:, four[c]], True, True)
            else:
                P.mm(ps[b][:, 0:128], Z[:, four[c]], vb[:, four[c]], True, False)
                P.wait(wt_ready, s_ready)
                m = P.mm_mark(ps[b][:, 0:128], wt[:, four[c]], St[:, 0:128], False, True)
            A.wait(m, y_read)
            u_ready = A.copy(U[:, four[c]], ps[b][:, 0:128])
            self.bank_read[b] = [u_ready]
            yield
            if c < 3:
                b = self.next_misc()
                P.wait(u_ready, kd_ready, *self.bank_read[b])
                m = P.mm_mark(ps[b][:, 0:128], kd[:, four[c]], U[:, four[c]], True, True)
            ob = self.next_misc()
            P.wait(u_ready, pt_ready, *self.bank_read[ob])
            if c == 0:
                o_done = P.mm_mark(ps[ob][:, 0:128], U[:, four[c]], pt[:, four[c]], True, True)
            else:
                P.wait(qg_ready)
                P.mm(ps[ob][:, 0:128], U[:, four[c]], pt[:, four[c]], True, False)
                o_done = P.mm_mark(ps[ob][:, 0:128], St[:, 0:128], Q[:, four[c]], False, True)
            A.wait(o_done, am_ready)
            o_ready = A.copy(o[:, four[c]], ps[ob][:, 0:128])
            self.bank_read[ob] = [o_ready]
            if c < 3:
                V.wait(m)
                if c:
                    V.wait(s_ready, o_done, eg_ready)
                    s_ready = V.stt(St[:, 0:128], St[:, 0:128], eg[:, 128 * c + 127:128 * c + 128],
                                    ps[b][:, 0:128], ALU.mult, ALU.add)
                else:
                    V.wait(am_read)
                    s_ready = V.copy(St[:, 0:128], ps[b][:, 0:128])
                self.bank_read[b] = [s_ready]
            yield
        while 4 + h not in self.gate_ready:
            yield
        A.wait(o_ready)
        squared = A.act(pt[:, :], o[:, :], ACT.Square)
        yield
        b = self.next_misc()
        P.wait(squared, *self.bank_read[b])
        for c in range(4):
            put = P.mm_mark if c == 3 else P.mm
            n = put(ps[b][:, c:c + 1], pt[:, four[c]], self.c("ones", 0, 1), True, True)
        root, rms = self.rstd_columns(ps[b], sd[:, 8:12], 128, n)
        self.bank_read[b] = [root]
        yield
        b = self.next_misc()
        P.wait(*self.bank_read[b])
        spread = self.rows_of(ps[b], sd[:, 8:12], rms)
        y_ready[4 + h] = self.gated_norm(o, o_ready, self.cl("g_out_norm", 4 * l + h), y[4 + h],
                                         self.gate_ready[4 + h], b, spread)
        self.heads_end += [P.here(), A.here(), V.here()]

    def second(self, gain):
        P, A, V, G = self.P, self.A, self.V, self.G
        self.fence()
        self.small_product()
        self.ring = (*B_MISC, B_SUM)

        def rows():
            nonlocal cs_ready, dt_ready, cc_ready
            dt, da, t1, t2, t3 = (self.at_slot(S_XP + n)[0:32, :] for n in range(5))
            V.wait(self.small_done)
            m = V.tt(dt, self.ps[B_ATT][0:32, :], self.rs[0:32, :], ALU.mult)
            self.bank_read[B_ATT] = [m]
            V.own()
            m = V.ts(dt, dt, self.cl("ssm_dt_bias_2", rows=32), ALU.add)
            sp = yield from self.softplus(dt, dt, t1, t2, t3, m)
            ea = A.act(self.one_col[0:32, :], self.cl("ssm_a_log_2", rows=32), ACT.Exp)
            V.wait(ea, sp)
            V.ts(da, dt, self.one_col[0:32, :], ALU.mult, -1.0, ALU.mult)
            V.own()
            cs = V.scan(t2, self.c("ones", 0, 1, rows=32).to_broadcast([32, 512]), da, ALU.mult, ALU.add)
            yield
            cs_ready = self.split_rows(cs_rows, t2, 32, cs)
            dt_ready = self.columns(dt_cols, dt, 32, sp)
            yield
            V.wait(self.columns(ncs_cols, t2, 32, cs))
            cc_ready = V.ts(ncs_cols, ncs_cols, -1.0, ALU.mult)

        cs_rows = self.at_slot(S_CS, dt=R)
        dt_cols, ncs_cols = self.columns_for(128), self.columns_for(128)
        cs_ready = dt_ready = cc_ready = None

        acc = [self.at_slot(S_ACC + i) for i in range(8)]
        self.acc_ready = [None] * 8
        x = [[self.at_slot(S_X[s] + i) for i in range(4)] for s in range(2)]
        z = [[self.at_slot(S_Z[s] + i) for i in range(4)] for s in range(2)]
        B, C, cb = self.at_slot(S_B), self.at_slot(S_C), self.at_slot(S_CB, 3)
        xp = [self.at_slot(S_XP + 2 * j, 2) for j in range(4)]
        bc_read = []
        out_read = [[], []]
        x_ready, z_ready, y_ready = {}, [{} for _ in range(4)], {}
        prepared, squares, squares_read = [], self.at_slot(S_SQ), []

        def load_bcx(g):
            for key, t, name in (("B", B, 16 + g), ("C", C, 20 + g)):
                A.wait(*bc_read)
                self.proj_h(1, conv_of(key, t, name))
            A.wait(*out_read[g % 2])
            for i in range(4):
                self.proj_h(1, conv_of(i, x[g % 2][i], 4 * g + i))

        def conv_of(key, t, name):
            got = {}
            x_ready[key] = got
            return self.conv(lambda _: t, got, lambda _, k: self.cl("ssm_conv_w_2", 24 * k + name),
                             lambda _: self.cl("ssm_conv_b_2", name), self.silu)

        def heads(g, xr):
            nonlocal bc_read
            s = g % 2
            bc = [x_ready["B"][0], x_ready["C"][0]]
            cb_free = V.here()
            for jt in range(4):
                w = T - 128 * jt
                b = self.next_misc()
                P.wait(*bc, *self.bank_read[b])
                m = P.mm_mark(self.ps[b][:, 0:w], B[:, 128 * jt:128 * jt + 128], C[:, 128 * jt:T], True, True)
                A.wait(m, cb_free)
                for t, at, n in PIECES[jt]:
                    cb_ready = A.copy(cb[:, at:at + n], self.ps[b][:, t - 128 * jt:t - 128 * jt + n])
                self.bank_read[b] = [cb_ready]
                if jt % 2:
                    yield
            bc_read = [m]
            prepared.append(g)
            for i in range(4):
                b, t = self.turn_tile(x[s][i], [xr[i]])
                V.wait(t, xp_zero, dt_ready)
                for j in range(4):
                    for q in range(2):
                        h = 2 * i + q
                        a = 32 * j + 8 * g + h
                        xp_ready = V.ts(xp[j][:, 128 * h + 64 * q:128 * h + 64 * q + 64],
                                        self.ps[b][:, 128 * j + 64 * q:128 * j + 64 * q + 64],
                                        dt_cols[:, a:a + 1], ALU.mult)
                self.bank_read[b] = [xp_ready]
                yield
            d = [self.at_slot(S_D[q], 3) for q in range(2)]
            d_read = [[], []]
            bank = self.ps[B_ATT]
            put_off, sums = [], []

            def weights(h):
                b, spread = self.spread(cs_rows, 8 * g + h, cs_ready)
                out = d[h % 2]
                col = lambda jt: ncs_cols[:, 32 * jt + 8 * g + h:32 * jt + 8 * g + h + 1]
                V.wait(spread, cc_ready, *d_read[h % 2])
                for jt in range(4):
                    m = V.stt(out[:, DIAG[jt]:DIAG[jt] + 128], self.ps[b][:, 128 * jt:128 * jt + 128], col(jt),
                              self.c("mask", 0, 128), ALU.add, ALU.min)
                A.wait(m)
                for jt in range(3):
                    w = T - 128 * jt - 128
                    r = A.act(out[:, REST[jt]:REST[jt] + w], self.ps[b][:, T - w:T], ACT.Exp, bias=col(jt))
                self.bank_read[b] = [m, r]
                return A.act(out[:, 0:512], out[:, 0:512], ACT.Exp)

            def weigh(h, e):
                V.wait(e, cb_ready)
                return V.tt(d[h % 2][:, 0:QW], d[h % 2][:, 0:QW], cb[:, 0:QW], ALU.mult)

            def gated(i, t, v):
                V.wait(v, z_ready[g][i])
                v = V.tt(t[:, :], t[:, :], z[s][i][:, :], ALU.mult)
                A.wait(v, *squares_read)
                return i, A.act(squares[:, :], t[:, :], ACT.Square)

            def sum_up(i, a):
                P.wait(a, *self.bank_read[B_SSM])
                for j in range(4):
                    n = P.mm_share(self.ps[B_SSM][:, j:j + 1], squares[:, 128 * j:128 * j + 128],
                                   self.c("ones", 0, 1), i == 0 and j == 0, i == 3, j == 3)
                squares_read[:] = [n]
                return n

            e = weights(0)
            yield
            w = weigh(0, e)
            yield
            for h in range(8):
                i, q = h // 2, h % 2
                e = weights(h + 1) if h < 7 else None
                P.wait(w, xp_ready, *self.bank_read[B_ATT])
                for jt in range(4):
                    for t, at, n in PIECES[jt]:
                        put = P.mm_mark if jt == 3 else P.mm
                        m = put(bank[:, t:t + n], xp[jt][:, 128 * h:128 * h + 128], d[q][:, at:at + n],
                                q == 0 and jt == 0, q == 1 and jt == 3)
                d_read[q] = [m]
                if sums:
                    n = sum_up(*sums.pop())
                yield
                if e:
                    w = weigh(h + 1, e)
                if q:
                    t = x[s][i]
                    V.wait(m, xr[i])
                    v = V.stt(t[:, :], t[:, :], self.cl("ssm_d_2", 4 * g + i), bank[:, :], ALU.mult, ALU.add)
                    self.bank_read[B_ATT] = [v]
                    put_off.append((i, t, v))
                if put_off and not sums:
                    sums.append(gated(*put_off.pop(0)))
                yield
            while put_off or sums:
                if sums:
                    n = sum_up(*sums.pop())
                if put_off:
                    sums.append(gated(*put_off.pop(0)))
                yield
            cols = self.d_cols[0][:, 8:12]
            root, ready = self.rstd_columns(self.ps[B_SSM], cols, 512, n)
            self.bank_read[B_SSM] = [root]
            yield
            b = self.next_misc()
            P.wait(*self.bank_read[b])
            spread = self.rows_of(self.ps[b], cols, ready)
            self.col_read = [spread]
            V.wait(spread)
            for i in range(4):
                t = x[s][i]
                v = V.stt(t[:, :], t[:, :], self.cl("ssm_norm_w_2", 4 * g + i), self.ps[b][:, :], ALU.mult, ALU.mult)
                hi, lo = self.at_slot(S_Z[s] + i, dt=R), self.at_slot(S_X[s] + i, dt=R)
                y_ready[g, i] = self.split_tile(t[:, :], hi[:, :], lo[:, :], v)
            self.bank_read[b] = [v]

        def out(g):
            s = g % 2
            xs = [(self.at_slot(S_Z[s] + i, dt=R), self.at_slot(S_X[s] + i, dt=R)) for i in range(4)]

            def take(i, bank, done):
                V.wait(done)
                if g == 0:
                    m = V.copy(acc[i][:, :], bank[:, :])
                else:
                    V.wait(self.acc_ready[i])
                    m = V.tt(acc[i][:, :], acc[i][:, :], bank[:, :], ALU.add)
                self.acc_ready[i] = m
                if g < 3:
                    return [m]
                V.wait(m, gate_ready[i])
                self.acc_ready[i] = V.tt(acc[i][:, :], acc[i][:, :], gate[i][:, :], ALU.mult)
                return [m]

            self.proj(8, xs, [y_ready[g, i] for i in range(4)], take)
            out_read[s] = [P.here()]

        def load_z(g):
            V.wait(*out_read[g % 2])
            self.proj_h(4, self.keep(lambda i: z[g % 2][i], z_ready[g],
                                     fn=lambda d, i: A.act(d[:, :], d[:, :], ACT.Silu)))

        self.pace = 0.3
        self.work.append(rows())
        load_bcx(0)
        load_z(0)
        self.finish()
        G.wait(P.here(), A.here(), V.here())
        for j in range(4):
            xp_zero = G.mark(lambda e, j=j: e.memset(xp[j][:, :], 0.0))
        self.pace = SSM_PACE
        for g in range(4):
            self.work.append(heads(g, [x_ready[i][0] for i in range(4)]))
            if g:
                out(g - 1)
            while g not in prepared:
                self.step()
            if g < 3:
                load_bcx(g + 1)
                load_z(g + 1)
            else:
                gate, gate_ready = [*x[0], *z[0]], {}
                V.wait(*out_read[0])
                self.proj_h(8, self.keep(lambda i: gate[i], gate_ready, fn=lambda d, i: A.act(
                    d[:, :], d[:, :], ACT.Sigmoid, bias=self.cl("b_branch_gate_2", i))))
            self.finish()
        self.pace = 0.0
        out(3)
        self.lru(acc, gain)

    def lru(self, acc, gain):
        P, A, V = self.P, self.A, self.V
        self.fence()
        self.ring = (*B_MISC, B_ATT, B_SSM, B_SUM)
        lam = self.columns_for(50)
        L = lambda j: lam[:, 10 * j:10 * j + 10]
        m = V.ts(L(0), self.cl("lru_lambda_2", 0, 10), -1.0, ALU.mult)
        drain(self.softplus(L(4), L(0), L(1), L(2), L(3), m))
        V.own()
        lam_ready = V.ts(L(0), L(4), 8.0, ALU.mult)
        V.wait(lam_ready)
        y = [(self.at_slot(L_Y + 2 * i, dt=R), self.at_slot(L_Y + 2 * i + 1, dt=R)) for i in range(10)]
        y_ready = [None] * 10
        r = [self.at_slot(L_R + i) for i in range(2)]
        gi = [self.at_slot(L_I + i) for i in range(2)]
        ends = [[], []]

        def scans(p, u, yl, yl_ready, g_ready, split):
            two = range(2)
            th, sq, tanh, a2, iu = {}, {}, {}, {}, {}
            for i in two:
                k = 2 * p + i
                th[i], sq[i] = self.next_tmp(), self.next_tmp()
                V.wait(g_ready[0, i])
                m = V.ts(r[i][:, :], r[i][:, :], lam[:, k:k + 1], ALU.mult)
                A.wait(m, *self.tmp_read[th[i][0]], *self.tmp_read[sq[i][0]])
                tanh[i] = A.act(th[i][1][:, :], r[i][:, :], ACT.Tanh)
                a = A.act(r[i][:, :], r[i][:, :], ACT.Exp, scale=-1.0)
                A.wait(a)
                a2[i] = A.act(sq[i][1][:, :], r[i][:, :], ACT.Square)
                V.wait(g_ready[1, i], *split[i])
                iu[i] = V.tt(gi[i][:, :], gi[i][:, :], u[i][:, :], ALU.mult)
            root = {}
            for i in two:
                t = th[i][1]
                V.wait(a2[i], tanh[i])
                m = V.stt(t[:, :], sq[i][1][:, :], 1.0, t[:, :], ALU.add, ALU.mult)
                self.tmp_read[sq[i][0]] = [m]
                A.wait(m)
                root[i] = A.act(t[:, :], t[:, :], ACT.Sqrt)
            for i in two:
                V.wait(root[i], iu[i])
                b = V.tt(gi[i][:, :], gi[i][:, :], th[i][1][:, :], ALU.mult)
                self.tmp_read[th[i][0]] = [b]
            yield
            for i in two:
                k = 2 * p + i
                V.own()
                h = V.scan(u[i][:, :], r[i][:, :], gi[i][:, :], ALU.mult, ALU.add)
                V.wait(h, yl_ready[i])
                m = V.tt(u[i][:, :], u[i][:, :], yl[i][:, :], ALU.mult)
                y_ready[k] = self.split_tile(u[i][:, :], y[k][0][:, :], y[k][1][:, :], m)
                yield
            ends[p % 2] = [V.here(), A.here()]

        uh = [(self.at_slot(L_UH + 2 * i, dt=R), self.at_slot(L_UH + 2 * i + 1, dt=R)) for i in range(2)]
        uh_read = []

        def gates(p, u, yl, yl_ready, split):
            nonlocal uh_read
            g_ready = {}
            for n, (dst, bias) in enumerate(((r, "lru_b_r_2"), (gi, "lru_b_i_2"))):
                wh, wl = self.unit()
                for i in range(2):
                    b = self.next_misc()
                    P.wait(*split[i], *self.bank_read[b])
                    m = P.mm3(self.ps[b][:, :], (wh[:, i, :], wl[:, i, :]), (uh[i][0][:, :], uh[i][1][:, :]),
                              True, True, True)
                    A.wait(m, *ends[1 - p % 2])
                    g_ready[n, i] = A.act(dst[i][:, :], self.ps[b][:, :], ACT.Sigmoid,
                                          bias=self.cl(bias, 2 * p + i))
                    self.bank_read[b] = [g_ready[n, i]]
                self.unit_used(m)
            uh_read = [m]
            self.work.append(scans(p, u, yl, yl_ready, g_ready, split))

        last = None
        self.pace = 0.25
        for p in range(5):
            s = p % 2
            u = [self.at_slot(L_U[s] + i) for i in range(2)]
            yl = [self.at_slot(L_YL[s] + i) for i in range(2)]
            A.wait(*ends[s])
            V.wait(*ends[s])
            got, yl_ready, split = {}, {}, {}
            self.proj_h(2, self.conv(lambda i: u[i], got, lambda i, k: self.cl("lru_conv_w_2", 10 * k + 2 * p + i),
                                     lambda i: self.cl("lru_conv_b_2", 2 * p + i)))
            self.finish()
            if last:
                gates(*last)
            A.wait(*uh_read)
            V.wait(*uh_read)
            for i in range(2):
                split[i] = self.split_tile(u[i][:, :], uh[i][0][:, :], uh[i][1][:, :], got[i])
            self.proj_h(2, self.keep(lambda i: yl[i], yl_ready, fn=lambda d, i: A.act(
                d[:, :], d[:, :], ACT.Gelu_apprx_tanh)))
            last = (p, u, yl, yl_ready, split)
        self.finish()
        gates(*last)
        gate = [self.at_slot(n) for n in (*L_GATE[1], *L_GATE[0])]
        gate_ready = [{}, {}]
        self.pace = 0.4
        for s in range(2):
            if s:
                self.finish()
                self.pace = 0.0
            for e in (A, V):
                e.wait(*ends[1 - s])
            self.proj_h(4, self.keep(lambda i: gate[4 * s + i], gate_ready[s], fn=lambda d, i: A.act(
                d[:, :], d[:, :], ACT.Sigmoid, bias=self.cl("b_branch_gate_2", 8 + 4 * s + i))))
        self.hn_last = P.here()
        V.wait(P.here(), A.here())
        A.wait(P.here())
        parts = [(self.at_slot(L_UH + i, dt=R), self.at_slot((*L_GATE[1], *L_GATE[0])[i], dt=R)) for i in range(8)]
        split = [None] * 8

        def take(i, bank, done):
            V.wait(done, gate_ready[i // 4][i % 4])
            m = V.tt(gate[i][:, :], gate[i][:, :], bank[:, :], ALU.mult)
            V.wait(m, self.acc_ready[i])
            c = V.tt(acc[i][:, :], acc[i][:, :], gate[i][:, :], ALU.add)
            split[i] = self.split_tile(acc[i][:, :], parts[i][0][:, :], parts[i][1][:, :], c)
            return [m]

        self.proj(8, y, y_ready, take)
        self.ring = B_MISC
        self.proj(8, parts, split, self.add_h(1.0, gain))

    def build(self):
        P, A, V, G, S, I = self.P, self.A, self.V, self.G, self.S, self.I
        self.rs, self.rc = self.at_slot(RSTD), self.columns_for(4)
        self.m_cols, self.g_cols, self.b_cols = (self.columns_for(16) for _ in range(3))
        self.one_col = self.columns_for(1)
        self.d_cols = [self.columns_for(12) for _ in range(2)]
        self.col_read, self.gate_ready = [], {}
        x = [self.at_slot(2 * j, 2) for j in range(4)]
        cst_ready = self.load("cst", self.cst[:, :], I["consts"])
        col_ready = self.load("col", self.col[:, :], I["cols"])
        xt = [self.load(f"x{j}", x[j][:, :], I["x"][128 * j:128 * j + 128, :], S if j < 2 else G) for j in range(4)]
        sel_ready = self.load("sel", self.at_slot(8)[:, 0:NSEL], I["sel"])
        for u in range(NRAW):
            self.fetch(u)
        for q in (P, A, V):
            q.wait(cst_ready, col_ready)
        gain = ("ffn1_norm", 0)
        self.hn_last = cst_ready
        P.wait(*xt)
        for i in range(8):
            b = B_MISC[i % 3]
            P.wait(*self.bank_read[b])
            for j in range(4):
                turn = P.turn_mark if j == 3 else P.turn
                t = turn(self.ps[b][:, 128 * j:128 * j + 128], x[j][:, 128 * i:128 * i + 128], self.c("ident"))
            self.run_late()
            V.wait(t)
            v = V.copy(self.h[i][:, :], self.ps[b][:, :])
            self.bank_read[b] = [v]
            self.h_new(i, v, gain)
            if i % 2:
                self.split(i // 2)
        A.wait(sel_ready)
        sel_ready = A.copy(self.selr[:, :], self.at_slot(8)[:, 0:NSEL])
        P.wait(sel_ready)
        for l in range(2):
            self.ffn(0.5, ("mix_norm", 8 * l))
            self.mixer(l, ("ffn2_norm", 8 * l))
            self.ffn(0.5, ("ffn1_norm", 8) if l == 0 else ("final_norm", 0))
        self.norm_h()
        for i in range(8):
            self.run_late()
            self.h_new(i, self.h_ready[i][0], ("norm1_w_2", 0))
        self.second(("norm2_w_2", 0))
        self.ffn(1.0, ("norm_f_w_2", 0))
        self.norm_h("norm_f_w_2")
        self.fence()
        for j in range(4):
            o = self.at_slot(2 * j, 2)
            for half in range(2):
                b = self.next_misc()
                P.wait(*self.bank_read[b])
                for i in range(4):
                    k = 4 * half + i
                    P.wait(*self.h_ready[k])
                    turn = P.turn_mark if i == 3 else P.turn
                    t = turn(self.ps[b][:, 128 * i:128 * i + 128], self.h[k][:, 128 * j:128 * j + 128],
                             self.c("ident"))
                if half:
                    A.wait(t)
                    self.bank_read[b] = [A.copy(o[:, 512:1024], self.ps[b][:, :])]
                else:
                    V.wait(t)
                    self.bank_read[b] = [V.copy(o[:, 0:512], self.ps[b][:, :])]
            S.wait(A.here(), V.here())
            S.put(lambda e, o=o, j=j: e.dma_start(self.out[128 * j:128 * j + 128, :], o[:, :]).then_inc(self.s_out, 16))
        S.wait((self.s_out, 64))

    def norm_h(self, name="final_norm"):
        self.norm_ready()
        for i in range(8):
            self.V.wait(*self.h_ready[i])
            self.h_ready[i] = [self.V.stt(self.h[i][:, :], self.h[i][:, :], self.cl(name, i), self.rs[:, :],
                                          ALU.mult, ALU.mult)]


def plan_units(ins):
    out = []

    def tiles(w, first, n):
        for i in range(first, first + n):
            width = w.shape[2]
            for a in range(0, width, 1024):
                b = min(a + 1024, width)
                out.append((w[i, :, a:b], b - a))

    def ffn(wg, g0, wu, u0, wd):
        for i in range(NH):
            tiles(wg, g0 + i, 1)
            tiles(wu, u0 + i, 1)
        tiles(wd, 0, 8)

    for l in range(2):
        ffn(ins["ffn1_w_gate"][l], 0, ins["ffn1_w_up"][l], 0, ins["ffn1_w_down"][l])
        w = ins["w_in"][l]
        out.append((ins["gate_w"][l], 1024))
        for half in range(2):
            for kind in range(3):
                tiles(w, 16 + 4 * kind + 2 * half, 2)
            if half == 0:
                tiles(w, 6, 2)
                tiles(w, 28, 2)
                tiles(w, 0, 6)
            else:
                tiles(w, 8, 8)
                tiles(w, 30, 2)
        tiles(ins["w_out"][l], 0, 8)
        ffn(ins["ffn2_w_gate"][l], 0, ins["ffn2_w_up"][l], 0, ins["ffn2_w_down"][l])
    w = ins["w_in_2"]
    out.append((ins["dt_w"], 1024))

    def bcx(g):
        tiles(w, 48 + g, 1)
        tiles(w, 52 + g, 1)
        tiles(w, 32 + 4 * g, 4)

    for g in range(5):
        if g > 1:
            tiles(ins["w_out_ssm_2"][g - 2], 0, 8)
        if g < 4:
            bcx(g)
            tiles(w, 16 + 4 * g, 4)
    tiles(w, 0, 8)
    tiles(ins["w_out_ssm_2"][3], 0, 8)
    for p in range(6):
        if p < 5:
            tiles(w, 56 + 2 * p, 2)
        if p:
            for m in ("lru_w_r_2", "lru_w_i_2"):
                out.append((ins[m][p - 1], 256))
        if p < 5:
            tiles(w, 66 + 2 * p, 2)
    tiles(w, 8, 8)
    tiles(ins["w_out_lru_2"], 0, 8)
    tiles(ins["w_out_2"], 0, 8)
    ffn(ins["w_ffn_in_2"], 0, ins["w_ffn_in_2"], NH, ins["w_ffn_out_2"])
    return out


def build_program(nc, ins, out):
    with ExitStack() as ctx:
        k = Kernel(nc, ins, out, ctx)
        k.build()
        assert len(k.unit_done) == len(k.units)
        block = ctx.enter_context(nc.Block())
        block.sync(k.S.run)
        block.gpsimd(k.G.run)
        block.scalar(k.A.run)
        block.vector(k.V.run)
        block.tensor(k.P.run)


def fill(table, width, parts):
    c = np.zeros((128, width), np.float32)
    for name, a in parts:
        o, w = table[name]
        c[:a.shape[0] if a.ndim else 128, o:o + w] = a
    return c


def consts():
    p = np.arange(128)
    lm = [(p[None, :] >> s == (p[:, None] >> s) + 1) & ((p[:, None] >> s) % 2 == 0) for s in range(7)]
    cst = fill(CONSTS, NCONST, (
        ("ident", np.eye(128)), ("ones", np.ones((128, 2))), ("bd64", p[:, None] // 64 == p[None, :] // 64),
        ("mask", np.where(np.arange(512)[None, :] >= p[:, None], 0.0, NEG)), ("lmask", np.concatenate(lm, axis=1))))
    sel = fill(SEL, NSEL, (
        ("row", p[:, None] % 32 == np.arange(32)[None, :]),
        ("pair", np.arange(256)[None, :] // 64 == p[:, None] % 32)))
    rot = np.zeros((128, 128))
    for m in range(128):
        rot[m + 32 if m % 64 < 32 else m - 32, m] = -1.0 if m % 64 < 32 else 1.0
    inv = np.float32(10000.0) ** (-np.arange(0, 64, 2, dtype=np.float32) / np.float32(64))
    ang = (np.arange(512, dtype=np.float32)[None, :] * inv[p % 32][:, None]).astype(np.float64)
    rope = fill(TABLES, NROPE, (("rot", rot), ("cos", np.cos(ang)), ("sin", np.sin(ang))))
    rel = np.arange(512)[None, :] - p[:, None]
    ret = np.stack([np.where(rel >= 0, np.exp(np.maximum(rel, 0) * np.log1p(-2.0 ** (-5.0 - h))), 0.0)
                    for h in range(4)]).astype(np.float32)
    return cst, sel, rope, ret


def small_columns(x):
    parts = [(n, x[n].reshape(-1, 128).T) for n in (
        "ffn1_norm", "mix_norm", "ffn2_norm", "final_norm", "m_out_norm", "r_out_norm", "g_out_norm", "g_conv",
        "norm1_w_2", "norm2_w_2", "norm_f_w_2", "b_branch_gate_2", "ssm_conv_w_2", "ssm_conv_b_2",
        "ssm_norm_w_2", "lru_conv_w_2", "lru_conv_b_2", "lru_b_r_2", "lru_b_i_2", "lru_lambda_2")]
    parts += [(n, x[n].T) for n in ("m_i_bias", "m_f_bias", "g_a_log", "g_dt_bias", "ssm_dt_bias_2", "ssm_a_log_2")]
    parts.append(("ssm_d_2", np.repeat(x["ssm_d_2"].reshape(-1), 64).reshape(-1, 128).T))
    parts.append(("eps", np.full((128, 1), EPS, np.float32)))
    return fill(COLS, NCOLS, parts)


def by_tiles(w):
    k, n = w.shape
    return w.reshape(k // 128, 128, n // 128, 128).transpose(2, 1, 0, 3).reshape(n // 128, 128, k)


def padded(w, parts):
    g = np.zeros((w.shape[0], 128), np.float32)
    for at, a, b in parts:
        g[:, at:at + b - a] = w[:, a:b]
    return by_tiles(g)[0]


def lay_out(x):
    both = lambda f: np.ascontiguousarray(np.stack([f(0), f(1)]))
    a = {n: both(lambda l: by_tiles(x[n][l])) for n in (
        "ffn1_w_gate", "ffn1_w_up", "ffn1_w_down", "w_out", "ffn2_w_gate", "ffn2_w_up", "ffn2_w_down")}
    w = x["w_in"]
    a["w_in"] = both(lambda l: np.concatenate(
        [by_tiles(w[l][:, 0:1024]), by_tiles(w[l][:, 1032:2056]), by_tiles(w[l][:, 2056:4104])]))
    a["gate_w"] = both(lambda l: padded(w[l], ((0, 1024, 1028), (32, 1028, 1032), (64, 4104, 4108),
                                               (96, 4108, 4112))))
    w = x["w_in_2"][0]
    a["w_in_2"] = np.concatenate([by_tiles(w[:, 0:7168]), by_tiles(w[:, 7200:9760])])
    a["dt_w"] = padded(w, ((0, 7168, 7200),))
    for n in ("w_out_lru_2", "w_out_2", "w_ffn_in_2", "w_ffn_out_2"):
        a[n] = np.ascontiguousarray(by_tiles(x[n][0]))
    a["w_out_ssm_2"] = np.stack([by_tiles(x["w_out_ssm_2"][0][512 * g:512 * g + 512]) for g in range(4)])
    for n in ("lru_w_r_2", "lru_w_i_2"):
        a[n] = np.ascontiguousarray(x[n][0].reshape(5, 2, 128, 128).transpose(0, 2, 1, 3).reshape(5, 128, 256))
    a["x"] = x["x"][0]
    a["consts"], a["sel"], a["rope"], a["ret"] = consts()
    a["cols"] = small_columns(x)
    return a


def kernel(**inputs):
    import concourse.bacc as bacc
    from concourse.bass_utils import run_bass_kernel_spmd

    arrays = lay_out({k: np.ascontiguousarray(v) for k, v in inputs.items()})
    nc = bacc.Bacc("TRN2", target_bir_lowering=False, num_devices=1)
    ins = {k: nc.dram_tensor(f"in_{k}", a.shape, F, kind="ExternalInput").ap() for k, a in arrays.items()}
    out = nc.dram_tensor("out_0", (T, D), F, kind="ExternalOutput").ap()
    build_program(nc, ins, out)
    r = run_bass_kernel_spmd(nc, [{f"in_{k}": a for k, a in arrays.items()}], core_ids=[0])
    return r.results[0]["out_0"].reshape(1, T, D)
```
